# Optimizing a Trainium2 kernel written in Bass

```python
import jax, jax.numpy as jnp
from jax import lax
import numpy as np

D_MODEL = 1024
BATCH = 1
SEQ = 512
DEPTH = 2

N_MIXERS = 2
N_HEADS = 16
HEAD_DIM = D_MODEL // N_HEADS
ATTN_WIDTH = N_HEADS * HEAD_DIM
Q_BLOCK = 128
POOL_WINDOWS = (2, 4, 8, 16)
N_POOL_GROUPS = len(POOL_WINDOWS)
POOL_GROUP_DIM = D_MODEL // N_POOL_GROUPS
D_FF = ((8 * D_MODEL // 3 + 255) // 256) * 256
N_ATTN_LAYERS = (DEPTH + 1) // 2
N_POOL_LAYERS = DEPTH // 2
EPS = 1e-6

kernel_name = "stickbreak_pool_interleaved_trunk"

def rmsnorm(x, g):
    xf = x.astype(jnp.float32)
    y = xf * lax.rsqrt(jnp.mean(xf * xf, axis=-1, keepdims=True) + EPS)
    return (y * g.astype(jnp.float32)).astype(x.dtype)

def stick_breaking_attention(h, w_qkv, q_gain, k_gain, w_o):
    B, S, _ = h.shape
    qkv = jnp.einsum('bsd,de->bse', h, w_qkv).reshape(B, S, 3, N_HEADS, HEAD_DIM)
    q = rmsnorm(qkv[:, :, 0], q_gain).transpose(0, 2, 1, 3)
    k = rmsnorm(qkv[:, :, 1], k_gain).transpose(0, 2, 1, 3)
    v = qkv[:, :, 2].transpose(0, 2, 1, 3)
    scale = HEAD_DIM ** -0.5
    n_blocks = S // Q_BLOCK
    q_blocks = q.reshape(B, N_HEADS, n_blocks, Q_BLOCK, HEAD_DIM).transpose(2, 0, 1, 3, 4)
    key_pos = jnp.arange(S)

    def one_block(args):
        q_blk, blk_idx = args
        q_pos = blk_idx * Q_BLOCK + jnp.arange(Q_BLOCK)
        z = jnp.einsum('bhqd,bhkd->bhqk', q_blk, k).astype(jnp.float32) * scale
        mask = key_pos[None, :] < q_pos[:, None]
        log_1m = jnp.where(mask, jax.nn.log_sigmoid(-z), 0.0)
        tail = lax.cumsum(log_1m, axis=3, reverse=True) - log_1m
        a = jnp.where(mask, jnp.exp(jax.nn.log_sigmoid(z) + tail), 0.0)
        return jnp.einsum('bhqk,bhkd->bhqd', a.astype(v.dtype), v)

    o = lax.map(one_block, (q_blocks, jnp.arange(n_blocks)))
    o = o.transpose(1, 3, 0, 2, 4).reshape(B, S, ATTN_WIDTH)
    return jnp.einsum('bse,ed->bsd', o, w_o)

def multiscale_pool_mixer(h, w_grp, scale):
    B, S, D = h.shape
    hf = h.astype(jnp.float32).reshape(B, S, N_POOL_GROUPS, POOL_GROUP_DIM)
    csum = jnp.cumsum(hf, axis=1)
    pos = jnp.arange(S)
    pooled = []
    for g, w in enumerate(POOL_WINDOWS):
        cg = csum[:, :, g]
        lagged = jnp.pad(cg, ((0, 0), (w, 0), (0, 0)))[:, :S]
        count = jnp.minimum(pos + 1, w).astype(jnp.float32)[None, :, None]
        pooled.append((cg - lagged) / count - hf[:, :, g])
    p = jnp.stack(pooled, axis=2).astype(h.dtype)
    y = jnp.einsum('bsgc,gce->bsge', p, w_grp).reshape(B, S, D)
    return y * scale

def swiglu_ffn(h, w_gu, w_down):
    gu = jnp.einsum('bsd,df->bsf', h, w_gu)
    gate, up = gu[..., :D_FF], gu[..., D_FF:]
    return jnp.einsum('bsf,fd->bsd', jax.nn.silu(gate) * up, w_down)

def setup_inputs(seed: int = 0) -> dict:
    key = jax.random.key(seed)
    ks = jax.random.split(key, 12)
    f32 = jnp.float32
    x = jax.random.normal(ks[0], (BATCH, SEQ, D_MODEL), f32)
    mix_norm = 1.0 + 0.02 * jax.random.normal(ks[1], (DEPTH, D_MODEL), f32)
    ffn_norm = 1.0 + 0.02 * jax.random.normal(ks[2], (DEPTH, D_MODEL), f32)
    attn_w_qkv = jax.random.normal(ks[3], (N_ATTN_LAYERS, D_MODEL, 3 * ATTN_WIDTH), f32) * D_MODEL ** -0.5
    attn_q_norm = 1.0 + 0.02 * jax.random.normal(ks[4], (N_ATTN_LAYERS, HEAD_DIM), f32)
    attn_k_norm = 1.0 + 0.02 * jax.random.normal(ks[5], (N_ATTN_LAYERS, HEAD_DIM), f32)
    attn_w_o = jax.random.normal(ks[6], (N_ATTN_LAYERS, ATTN_WIDTH, D_MODEL), f32) * ATTN_WIDTH ** -0.5
    pool_w = jax.random.normal(ks[7], (N_POOL_LAYERS, N_POOL_GROUPS, POOL_GROUP_DIM, POOL_GROUP_DIM), f32) * POOL_GROUP_DIM ** -0.5
    pool_scale = 1.0 + 0.02 * jax.random.normal(ks[8], (N_POOL_LAYERS, D_MODEL), f32)
    ffn_w_gu = jax.random.normal(ks[9], (DEPTH, D_MODEL, 2 * D_FF), f32) * D_MODEL ** -0.5
    ffn_w_down = jax.random.normal(ks[10], (DEPTH, D_FF, D_MODEL), f32) * D_FF ** -0.5
    return {"x": x, "mix_norm": mix_norm, "ffn_norm": ffn_norm,
            "attn_w_qkv": attn_w_qkv, "attn_q_norm": attn_q_norm, "attn_k_norm": attn_k_norm,
            "attn_w_o": attn_w_o, "pool_w": pool_w, "pool_scale": pool_scale,
            "ffn_w_gu": ffn_w_gu, "ffn_w_down": ffn_w_down}

def reference(x, mix_norm, ffn_norm, attn_w_qkv, attn_q_norm, attn_k_norm, attn_w_o,
              pool_w, pool_scale, ffn_w_gu, ffn_w_down):
    for i in range(DEPTH):
        j = i // N_MIXERS
        h = rmsnorm(x, mix_norm[i])
        if i % N_MIXERS == 0:
            x = x + stick_breaking_attention(h, attn_w_qkv[j], attn_q_norm[j], attn_k_norm[j], attn_w_o[j])
        else:
            x = x + multiscale_pool_mixer(h, pool_w[j], pool_scale[j])
        h = rmsnorm(x, ffn_norm[i])
        x = x + swiglu_ffn(h, ffn_w_gu[i], ffn_w_down[i])
    return x


_drawn_inputs = setup_inputs


def setup_inputs(seed=0):
    import zlib

    import numpy as np

    out = dict(_drawn_inputs(seed))
    spreads = {}
    factors = {'mix_norm': 2.856,
     'ffn_norm': 3.239,
     'attn_q_norm': 8.0,
     'attn_k_norm': 8.0,
     'pool_scale': 5.133}
    for name, (base, spread) in spreads.items():
        noise = np.random.default_rng([zlib.crc32(name.encode()), seed]).standard_normal(out[name].shape)
        drawn = base * np.exp(spread * noise) if base else spread * noise
        out[name] = __import__('jax').numpy.asarray(drawn.astype(out[name].dtype))
    for name, factor in factors.items():
        out[name] = (out[name] * factor).astype(out[name].dtype)
    return out
```

```python
from contextlib import ExitStack

import numpy as np

import concourse.bass as bass
from concourse import mybir

F32, F32R, BF16, I32 = mybir.dt.float32, mybir.dt.float32r, mybir.dt.bfloat16, mybir.dt.int32
ALU, ACT = mybir.AluOpType, mybir.ActivationFunctionType

P = 128
D, SEQ, HEADS, HD = 1024, 512, 16, 64
DFF = 2816
EPS = 1e-6
KT = D // P
FT = DFF // P
QB = SEQ // P
PAIRS = HEADS // 2
WINDOWS = (2, 4, 8, 16)
PAD = max(WINDOWS)
UK = 8
DOWN_UNITS = ((0, 8), (8, 16), (16, FT))
MASKED = -1e30

ZOFF = (0, 512, 1024, 896)
ZW = tuple(SEQ - P * i for i in range(QB))
ZCOLS = sum(ZW)

USE_WO = PAIRS
USE_GU = (USE_WO + KT // 2, USE_WO + KT // 2 + FT + KT + 1)
USE_DOWN = (USE_GU[0] + FT, USE_GU[1] + FT)
USE_POOL = USE_DOWN[0] + KT
USE_DOWN2 = (PAIRS, PAIRS + KT)
RES_WO, RES_DOWN, RES_POOL = 0, (KT, 3 * KT), 2 * KT
V_MIX, V_FFN, V_SCALE, V_Q, V_K = 0, 2 * KT, 4 * KT, 5 * KT, 5 * KT + 1


def build(nc, x_in, vec_in, inv_in, wqkv, wo, wgu, wdown, wpool, out):
    ctx = ExitStack()

    def sb(name, shape, dt=F32, where=ctx):
        return where.enter_context(nc.sbuf_tensor(name, shape, dt))

    def sem(name):
        return ctx.enter_context(nc.semaphore(name))

    with ctx:
        X = sb("X", [P, KT, SEQ])
        HH = sb("HH", [P, KT, SEQ], F32R)
        HL = sb("HL", [P, KT, SEQ], F32R)
        RAW = [sb(f"RAW{s}", [P, UK * P]) for s in range(3)]
        WH = [sb(f"WH{s}", [P, UK * P], F32R) for s in range(3)]
        WL = [sb(f"WL{s}", [P, UK * P], F32R) for s in range(3)]
        R = sb("R", [P, SEQ])
        SQ = sb("SQ", [P, SEQ])
        SQSUM = sb("SQSUM", [P, SEQ])
        VEC = sb("VEC", [P, 5 * KT + 2])
        INV = sb("INV", [P, len(WINDOWS), 1, PAD])
        EPSC = sb("EPSC", [P, 1])
        ONES = sb("ONES", [P, P])
        PAIRONES = sb("PAIRONES", [P, P])
        IDENT = sb("IDENT", [P, P])
        IDENTB = sb("IDENTB", [P, P], BF16)
        MASKB = sb("MASKB", [P, P], BF16)
        TRIF = sb("TRIF", [P, P])
        NEGTRI = sb("NEGTRI", [P, P], F32R)
        NEGONES = sb("NEGONES", [P, P], F32R)
        with ExitStack() as start:
            XSQ = sb("XSQ", [P, KT, SEQ], where=start)
            HF0 = sb("HF0", [P, KT, SEQ], where=start)
        with ExitStack() as attn:
            OH = sb("OH", [P, PAIRS, SEQ], F32R, attn)
            OL = sb("OL", [P, PAIRS, SEQ], F32R, attn)
            QKF = [sb(f"{n}F", [P, SEQ], where=attn) for n in "QK"]
            QKH = [sb(f"{n}H", [P, SEQ], F32R, attn) for n in "QK"]
            QKL = [sb(f"{n}L", [P, SEQ], F32R, attn) for n in "QK"]
            VT = sb("VT", [P, SEQ], where=attn)
            VH = sb("VH", [P, QB, 4, HD], F32R, attn)
            VL = sb("VL", [P, QB, 4, HD], F32R, attn)
            RS = sb("RS", [P, SEQ], where=attn)
            E = [sb(f"E{h}", [P, ZCOLS], where=attn) for h in range(2)]
            SP = [sb(f"SP{h}", [P, ZCOLS], where=attn) for h in range(2)]
            AH = [sb(f"AH{h}", [P, ZCOLS], F32R, attn) for h in range(2)]
            AL = [sb(f"AL{h}", [P, ZCOLS], F32R, attn) for h in range(2)]
        with ExitStack() as ffn:
            FH = sb("FH", [P, FT, SEQ], F32R, ffn)
            FL = sb("FL", [P, FT, SEQ], F32R, ffn)
            G = sb("G", [P, SEQ], where=ffn)
            S = sb("S", [P, SEQ], where=ffn)
            U = sb("U", [P, SEQ], where=ffn)
            A = sb("A", [P, SEQ], where=ffn)
        Y = [G, S]
        with ExitStack() as pool_mix:
            HP = sb("HP", [P, KT, PAD + SEQ], where=pool_mix)
            WIN = [sb(f"WIN{i}", [P, 2, PAD + SEQ], where=pool_mix) for i in range(2)]
            WINP = [sb(f"WINP{i}", [P, 2, PAD + SEQ], where=pool_mix) for i in range(2)]
            PD = [sb(f"PD{i}", [P, 2, SEQ], where=pool_mix) for i in range(2)]
            W16 = sb("W16", [P, 2, PAD], where=pool_mix)

        PS = ctx.enter_context(nc.psum_tensor("PS", [P, 8 * 512], F32))

        def bank(b, n=1):
            return PS[:, b * 512:(b + n) * 512]

        def ref_order(row):
            return row.rearrange("p (r b) -> p b r", b=QB)

        def by_block(row):
            return row.rearrange("p (b r) -> p b r", b=QB)

        Z = [bank(0, 3)[:, 0:ZCOLS], bank(3, 3)[:, 0:ZCOLS]]
        PROJ, MISC = bank(6), bank(7)
        RES = [bank(6), bank(5)]
        GATE, UP = bank(0), bank(1)

        x_loaded = [sem(f"x_loaded{i}") for i in range(4)]
        vec_loaded, inv_loaded = sem("vec_loaded"), sem("inv_loaded")
        raw_full = [sem(f"raw_full{s}") for s in range(3)]
        hi_ready = [sem(f"hi_ready{s}") for s in range(3)]
        lo_ready = [sem(f"lo_ready{s}") for s in range(3)]
        unit_done = [sem(f"unit_done{s}") for s in range(3)]
        stored = [sem(f"stored{i}") for i in range(2)]
        made, const_ready, tri_ready, vzero = sem("made"), sem("const_ready"), sem("tri_ready"), sem("vzero")
        eps_ready, gain_ready, ones_ready = sem("eps_ready"), sem("gain_ready"), sem("ones_ready")
        xsq_done, stats_done, ln_done, r_ready = sem("xsq_done"), sem("stats_done"), sem("ln_done"), sem("r_ready")
        hf_done, hh_done, hl_done = sem("hf_done"), sem("hh_done"), sem("hl_done")
        sq_one, sqsum_done = sem("sq_one"), sem("sqsum_done")
        resid_done = sem("resid_done")
        proj_copied, qksq_done, norm_done = sem("proj_copied"), sem("qksq_done"), sem("norm_done")
        rs_done, qkn_done, qkh_done, qkl_done = sem("rs_done"), sem("qkn_done"), sem("qkh_done"), sem("qkl_done")
        misc_read = sem("misc_read")
        vt_done, vh_done = sem("vt_done"), sem("vh_done")
        z_done, abs_done, exp_done, l_done = sem("z_done"), sem("abs_done"), sem("exp_done"), sem("l_done")
        sp_done, sph_done, spl_done, tail_done = sem("sp_done"), sem("sph_done"), sem("spl_done"), sem("tail_done")
        prob_done, ph_done, pl_done = sem("prob_done"), sem("ph_done"), sem("pl_done")
        o_done, oh_done = sem("o_done"), sem("oh_done")
        g_done, s_done, u_done, a_done = sem("g_done"), sem("s_done"), sem("u_done"), sem("a_done")
        fh_done, fl_done = sem("fh_done"), sem("fl_done")
        hp_done, padz, win_done, winp_done = sem("hp_done"), sem("padz"), sem("win_done"), sem("winp_done")
        pd_done, pdh_done, pdl_done, pool_done = sem("pd_done"), sem("pdh_done"), sem("pdl_done"), sem("pool_done")

        block = ctx.enter_context(nc.Block())

        @block.sync
        def _(sp):
            def load(slot, use, src, tiles=UK):
                if not (isinstance(use, int) and use == 0):
                    sp.wait_ge(lo_ready[slot], use)
                sp.dma_start(RAW[slot][:, 0:tiles * P], src).then_inc(raw_full[slot], 16)

            sp.dma_start(VEC[:], vec_in).then_inc(vec_loaded, 16)
            for i in range(4):
                sp.dma_start(X[:, 2 * i:2 * i + 2, :], x_in[:, 2 * i:2 * i + 2, :]).then_inc(x_loaded[i], 16)
            for j in range(3):
                load(j, 0, wqkv[0, j])
            sp.dma_start(INV[:], inv_in).then_inc(inv_loaded, 16)
            with sp.Fori(1, PAIRS) as n:
                for j in range(3):
                    load(j, n, wqkv[n, j])
            with sp.Fori(0, KT // 2) as i:
                for j in range(2):
                    load(j, i + USE_WO, wo[i, j])
            for layer in range(2):
                with sp.Fori(0, FT) as f:
                    for j in range(2):
                        load(j, f + USE_GU[layer], wgu[layer, f, j])
                with sp.Fori(0, KT) as c:
                    for j, (k0, k1) in enumerate(DOWN_UNITS):
                        use = c + (USE_DOWN2[layer] if j == 2 else USE_DOWN[layer])
                        load(j, use, wdown[layer, c, :, k0 * P:k1 * P], k1 - k0)
                if layer == 0:
                    for j in range(2):
                        load(j, USE_POOL, wpool[j])

        @block.gpsimd
        def _(pool):
            nc.gpsimd.memset(IDENT[:], 0.0).then_inc(made, 1)
            nc.gpsimd.memset(IDENTB[:], 0.0).then_inc(made, 1)
            nc.gpsimd.memset(MASKB[:], MASKED).then_inc(made, 1)
            nc.gpsimd.memset(TRIF[:], -1.0).then_inc(made, 1)
            nc.gpsimd.memset(PAIRONES[:], 0.0).then_inc(made, 1)
            pool.wait_ge(made, 5)
            for t in (IDENT, IDENTB):
                nc.gpsimd.affine_select(out=t[:], in_=t[:], compare_op=ALU.not_equal, fill=1.0, base=0,
                                        pattern=[[-1, P]], channel_multiplier=1).then_inc(const_ready, 1)
            nc.gpsimd.affine_select(out=MASKB[:], in_=MASKB[:], compare_op=ALU.is_ge, fill=0.0, base=0,
                                    pattern=[[-1, P]], channel_multiplier=1).then_inc(const_ready, 1)
            nc.gpsimd.affine_select(out=TRIF[:], in_=TRIF[:], compare_op=ALU.is_ge, fill=0.0, base=0,
                                    pattern=[[-1, P]], channel_multiplier=1).then_inc(const_ready, 1)
            for h in range(2):
                pool.wait_ge(const_ready, 4 + h)
                nc.gpsimd.memset(PAIRONES[h * HD:(h + 1) * HD, h * HD:(h + 1) * HD], 1.0).then_inc(const_ready, 1)
            pool.wait_ge(hl_done, KT)
            nc.gpsimd.memset(VH[:].bitcast(F32), 0.0).then_inc(vzero, 1)
            nc.gpsimd.memset(VL[:].bitcast(F32), 0.0).then_inc(vzero, 1)

            def qk_square(n, j):
                pool.wait_ge(proj_copied, 3 * n + (j + 1))
                if not (isinstance(n, int) and 2 * n + j == 0):
                    pool.wait_ge(norm_done, 2 * n + j)
                nc.gpsimd.tensor_tensor(SQ[:], QKF[j][:], QKF[j][:], ALU.mult).then_inc(qksq_done, 1)

            def qk_lo(n, j):
                pool.wait_ge(qkh_done, 2 * n + (j + 1))
                nc.gpsimd.tensor_tensor(QKL[j][:], QKF[j][:], QKH[j][:].bitcast(F32), ALU.subtract)\
                    .then_inc(qkl_done, 1)

            def qk_lane(n):
                qk_square(n, 0)
                qk_square(n, 1)
                qk_lo(n, 0)
                qk_lo(n, 1)

            qk_lane(0)
            with pool.Fori(1, PAIRS) as n:
                qk_lane(n)

            def square_sum(round_, first, tiles):
                if round_ == 0:
                    pool.wait_ge(norm_done, 2 * PAIRS)
                else:
                    pool.wait_ge(stats_done, round_ + 1)
                nc.gpsimd.memset(SQSUM[:], 0.0).then_inc(sqsum_done, 1)
                with pool.Fori(0, tiles) as c:
                    pool.wait_ge(sqsum_done, c + ((KT + 1) * round_ + 1))
                    pool.wait_ge(resid_done, c + (first + 1))
                    pool.wait_ge(vec_loaded, 16)
                    nc.gpsimd.tensor_tensor(SQ[:], X[:, c, :], X[:, c, :], ALU.mult).then_inc(sq_one, 1)
                    pool.wait_ge(sq_one, c + (KT * round_ + 1))
                    nc.gpsimd.tensor_tensor(SQSUM[:], SQSUM[:], SQ[:], ALU.add).then_inc(sqsum_done, 1)

            def ffn_mul(layer):
                with pool.Fori(0, FT) as f:
                    pool.wait_ge(s_done, f + (FT * layer + 1))
                    pool.wait_ge(u_done, f + (FT * layer + 1))
                    nc.gpsimd.tensor_tensor(A[:], U[:], S[:], ALU.mult).then_inc(a_done, 1)

            square_sum(0, RES_WO, KT)
            ffn_mul(0)
            square_sum(1, RES_DOWN[0], KT)
            pool.wait_ge(unit_done[2], USE_DOWN2[0] + KT)
            for t in (HP, *WIN, *WINP):
                nc.gpsimd.memset(t[:, :, 0:PAD], 0.0).then_inc(padz, 1)
            pool.wait_ge(padz, 5)
            g = len(WINDOWS) - 1
            pool.wait_ge(hp_done, 2)
            src = HP[:, 2 * g:2 * g + 2, :]
            for lv in range(g + 1):
                if lv:
                    pool.wait_ge(winp_done, lv)
                sh = 1 << lv
                nc.gpsimd.tensor_tensor(WINP[lv % 2][:, :, PAD:], src[:, :, PAD:], src[:, :, PAD - sh:PAD + SEQ - sh],
                                        ALU.add).then_inc(winp_done, 1)
                src = WINP[lv % 2]
            square_sum(2, RES_POOL, KT)
            ffn_mul(1)

        @block.scalar
        def _(act):
            def hi(slot, use):
                act.wait_ge(raw_full[slot], 16 * use + 16)
                if not (isinstance(use, int) and use == 0):
                    act.wait_ge(unit_done[slot], use)
                nc.scalar.activation(WH[slot][:], RAW[slot][:], ACT.Copy).then_inc(hi_ready[slot], 1)

            def inverse_rms(src, n, round_):
                act.wait_ge(stats_done, round_ + 1)
                nc.scalar.activation(R[:], src, ACT.Ln, bias=EPSC[:], scale=1.0 / n).then_inc(ln_done, 1)
                act.wait_ge(ln_done, round_ + 1)
                nc.scalar.activation(R[:], R[:], ACT.Exp, scale=-0.5).then_inc(r_ready, 1)

            nc.scalar.preload_act_table_set("natural_log_exp_and_others")
            act.wait_ge(eps_ready, 1)
            for k in range(KT):
                act.wait_ge(x_loaded[k // 2], 16)
                nc.scalar.activation(XSQ[:, k, :], X[:, k, :], ACT.Square).then_inc(xsq_done, 1)
            act.wait_ge(const_ready, 6)
            nc.scalar.activation(NEGTRI[:], TRIF[:], ACT.Copy).then_inc(tri_ready, 1)
            hi(0, 0)
            inverse_rms(bank(0), D, 0)
            for k in range(KT):
                act.wait_ge(hf_done, k + 1)
                nc.scalar.activation(HH[:, k, :], HF0[:, k, :], ACT.Copy).then_inc(hh_done, 1)
            hi(1, 0)
            hi(2, 0)

            def copy_qk(n, j):
                act.wait_ge(unit_done[j], n + 1)
                if not isinstance(n, int):
                    act.wait_ge(qkl_done, 2 * n + (j - 1))
                nc.scalar.activation(QKF[j][:], PROJ, ACT.Copy).then_inc(proj_copied, 1)

            def copy_v(n):
                act.wait_ge(unit_done[2], n + 1)
                if isinstance(n, int):
                    act.wait_ge(vzero, 2)
                nc.scalar.activation(VT[:], PROJ, ACT.Copy).then_inc(proj_copied, 1)

            def qk_rms(n, j):
                act.wait_ge(norm_done, 2 * n + (j + 1))
                if not (isinstance(n, int) and 2 * n + j == 0):
                    act.wait_ge(qkn_done, 2 * n + j)
                nc.scalar.activation(RS[:], MISC, ACT.Ln, bias=EPSC[:], scale=1.0 / HD).then_inc(misc_read, 1)
                act.wait_ge(misc_read, j + 1 if isinstance(n, int) else 4 * n + j)
                nc.scalar.activation(RS[:], RS[:], ACT.Exp, scale=-0.5).then_inc(rs_done, 1)

            def qk_hi(n, j):
                act.wait_ge(qkn_done, 2 * n + (j + 1))
                nc.scalar.activation(QKH[j][:], QKF[j][:], ACT.Copy).then_inc(qkh_done, 1)

            copy_qk(0, 0)
            hi(0, 1)
            copy_qk(0, 1)
            qk_rms(0, 0)
            qk_hi(0, 0)
            copy_v(0)
            qk_rms(0, 1)
            qk_hi(0, 1)

            def softplus_parts(a, h):
                act.wait_ge(abs_done, 2 * a + (h + 1))
                nc.scalar.activation(E[h][:], E[h][:], ACT.Exp, scale=-1.0).then_inc(exp_done, 1)
                act.wait_ge(exp_done, 2 * a + (h + 1))
                nc.scalar.activation(E[h][:], E[h][:], ACT.Ln, bias=1.0).then_inc(l_done, 1)

            def v_hi(a):
                act.wait_ge(vt_done, a + 1)
                nc.scalar.activation(VH[:, :, 0:4:3, :], MISC.rearrange("p (b h d) -> p b h d", b=QB, h=2),
                                     ACT.Copy).then_inc(vh_done, 1)

            def probs(a, h):
                act.wait_ge(tail_done, 2 * a + (h + 1))
                nc.scalar.activation(E[h][:], Z[h], ACT.Exp).then_inc(prob_done, 1)

            def o_hi(a):
                act.wait_ge(o_done, a + 1)
                act.wait_ge(vec_loaded, 16)
                nc.scalar.activation(ref_order(OH[:, a, :]), by_block(MISC), ACT.Copy).then_inc(oh_done, 1)

            with act.Fori(0, PAIRS - 1) as a:
                n = a + 1
                hi(1, n)
                softplus_parts(a, 0)
                softplus_parts(a, 1)
                hi(2, n)
                copy_qk(n, 0)
                v_hi(a)
                hi(0, n + 1)
                copy_qk(n, 1)
                qk_rms(n, 0)
                probs(a, 0)
                qk_hi(n, 0)
                probs(a, 1)
                qk_rms(n, 1)
                qk_hi(n, 1)
                copy_v(n)
                o_hi(a)
            a = PAIRS - 1
            hi(1, USE_WO)
            softplus_parts(a, 0)
            softplus_parts(a, 1)
            v_hi(a)
            probs(a, 0)
            probs(a, 1)
            o_hi(a)

            def next_hi(c, first, gains):
                act.wait_ge(resid_done, c + (first + 1))
                act.wait_ge(vec_loaded, 16)
                nc.scalar.activation(HH[:, c, :], X[:, c, :], ACT.Copy, scale=VEC[:, bass.ds(gains + c, 1)])\
                    .then_inc(hh_done, 1)

            def wo_pair(i, prepared=False):
                if not prepared:
                    hi(1, i + USE_WO)
                hi(0, i + (USE_WO + 1))
                next_hi(2 * i, RES_WO, V_FFN)
                next_hi(2 * i + 1, RES_WO, V_FFN)

            wo_pair(0, prepared=True)
            with act.Fori(1, KT // 2) as i:
                wo_pair(i)

            def f_hi(layer, f):
                act.wait_ge(a_done, f + (FT * layer + 1))
                act.wait_ge(vec_loaded, 16)
                nc.scalar.activation(FH[:, f, :], A[:], ACT.Copy).then_inc(fh_done, 1)

            def gate_up(layer, f):
                hi(1, f + USE_GU[layer])
                if not (isinstance(f, int) and f == 0):
                    f_hi(layer, f - 1)
                if isinstance(f, int):
                    inverse_rms(MISC, D, layer * 2 + 1)
                act.wait_ge(g_done, f + (FT * layer + 1))
                nc.scalar.activation(S[:], G[:], ACT.Silu).then_inc(s_done, 1)
                hi(0, f + (USE_GU[layer] + 1))

            def ffn(layer):
                gate_up(layer, 0)
                with act.Fori(1, FT) as f:
                    gate_up(layer, f)
                f_hi(layer, FT - 1)

                def down(c, last=False):
                    hi(1, c + USE_DOWN[layer])
                    hi(2, c + USE_DOWN2[layer])
                    if not last:
                        hi(0, c + (USE_DOWN[layer] + 1))

                def store(c, j):
                    act.wait_ge(resid_done, c + (RES_DOWN[1] + 1))
                    act.dma_start(out[:, c, :], Y[j][:]).then_inc(stored[j], 16)

                if layer == 0:
                    with act.Fori(0, KT) as c:
                        down(c)
                else:
                    with act.Fori(0, KT // 2 - 1) as i:
                        for j in range(2):
                            down(2 * i + j)
                            store(2 * i + j, j)
                    for j in range(2):
                        down(KT - 2 + j, last=j == 1)
                        store(KT - 2 + j, j)
                    for j in range(2):
                        act.wait_ge(stored[j], 16 * (KT // 2))

            ffn(0)
            hi(1, USE_POOL)
            inverse_rms(MISC, D, 2)
            for g in range(len(WINDOWS)):
                act.wait_ge(pd_done, g + 1)
                nc.scalar.activation(HH[:, 2 * g:2 * g + 2, :], PD[g % 2][:], ACT.Copy).then_inc(pdh_done, 1)
                if g:
                    for c in (2 * g - 2, 2 * g - 1):
                        act.wait_ge(pool_done, 2 * g)
                        next_hi(c, RES_POOL, V_FFN + KT)
            hi(0, USE_POOL + 1)
            for c in (KT - 2, KT - 1):
                act.wait_ge(unit_done[1], USE_POOL + 1)
                next_hi(c, RES_POOL, V_FFN + KT)
            ffn(1)

        @block.vector
        def _(dve):
            def lo(slot, use):
                dve.wait_ge(hi_ready[slot], use + 1)
                nc.vector.tensor_tensor(WL[slot][:], RAW[slot][:], WH[slot][:].bitcast(F32), ALU.subtract)\
                    .then_inc(lo_ready[slot], 1)

            nc.vector.memset(EPSC[:], EPS).then_inc(eps_ready, 1)
            nc.vector.memset(ONES[:], 1.0).then_inc(ones_ready, 1)
            nc.vector.memset(NEGONES[:].bitcast(F32), -1.0).then_inc(tri_ready, 1)
            dve.wait_ge(vec_loaded, 16)
            nc.vector.tensor_scalar(VEC[:, V_Q:V_Q + 1], VEC[:, V_Q:V_Q + 1], HD ** -0.5, None, ALU.mult)\
                .then_inc(gain_ready, 1)
            lo(0, 0)
            dve.wait_ge(r_ready, 1)

            def start_hi(k):
                nc.vector.scalar_tensor_tensor(HF0[:, k, :], X[:, k, :], VEC[:, V_MIX + k:V_MIX + k + 1], R[:],
                                               ALU.mult, ALU.mult).then_inc(hf_done, 1)

            def start_lo(k):
                dve.wait_ge(hh_done, k + 1)
                nc.vector.tensor_tensor(HL[:, k, :], HF0[:, k, :], HH[:, k, :].bitcast(F32), ALU.subtract)\
                    .then_inc(hl_done, 1)

            start_hi(0)
            for k in range(1, KT):
                start_hi(k)
                start_lo(k - 1)
            start_lo(KT - 1)
            lo(1, 0)
            lo(2, 0)
            lo(0, 1)

            def qk_norm(n, j):
                dve.wait_ge(rs_done, 2 * n + (j + 1))
                dve.wait_ge(gain_ready, 1)
                nc.vector.scalar_tensor_tensor(QKF[j][:], QKF[j][:], VEC[:, V_Q + j:V_Q + j + 1], RS[:],
                                               ALU.mult, ALU.mult).then_inc(qkn_done, 1)

            qk_norm(0, 0)
            qk_norm(0, 1)

            def score_abs(a, h):
                dve.wait_ge(z_done, 2 * a + (h + 1))
                nc.vector.tensor_scalar(E[h][:].bitcast(I32), Z[h].bitcast(I32), 0x7FFFFFFF, None, ALU.bitwise_and)\
                    .then_inc(abs_done, 1)

            def softplus(a, h):
                dve.wait_ge(l_done, 2 * a + (h + 1))
                nc.vector.scalar_tensor_tensor(SP[h][:], Z[h], 0.0, E[h][:], ALU.max, ALU.add).then_inc(sp_done, 1)
                dve.wait_ge(sp_done, 2 * a + (h + 1))
                nc.vector.tensor_copy(AH[h][:], SP[h][:]).then_inc(sph_done, 1)
                dve.wait_ge(sph_done, 2 * a + (h + 1))
                nc.vector.tensor_tensor(AL[h][:], SP[h][:], AH[h][:].bitcast(F32), ALU.subtract).then_inc(spl_done, 1)

            def v_lo(a):
                dve.wait_ge(vh_done, a + 1)
                nc.vector.tensor_tensor(VL[:, :, 0:4:3, :], MISC.rearrange("p (b h d) -> p b h d", b=QB, h=2),
                                        VH[:, :, 0:4:3, :].bitcast(F32), ALU.subtract).then_inc(misc_read, 1)

            def probs_split(a, h):
                dve.wait_ge(prob_done, 2 * a + (h + 1))
                nc.vector.tensor_copy(AH[h][:], E[h][:]).then_inc(ph_done, 1)
                dve.wait_ge(ph_done, 2 * a + (h + 1))
                nc.vector.tensor_tensor(AL[h][:], E[h][:], AH[h][:].bitcast(F32), ALU.subtract).then_inc(pl_done, 1)

            def o_lo(a):
                dve.wait_ge(oh_done, a + 1)
                nc.vector.tensor_tensor(ref_order(OL[:, a, :]), by_block(MISC), ref_order(OH[:, a, :].bitcast(F32)),
                                        ALU.subtract)\
                    .then_inc(misc_read, 1)

            with dve.Fori(0, PAIRS - 1) as a:
                n = a + 1
                lo(1, n)
                score_abs(a, 0)
                score_abs(a, 1)
                softplus(a, 0)
                softplus(a, 1)
                lo(2, n)
                v_lo(a)
                lo(0, n + 1)
                qk_norm(n, 0)
                probs_split(a, 0)
                probs_split(a, 1)
                qk_norm(n, 1)
                o_lo(a)
            a = PAIRS - 1
            lo(1, USE_WO)
            score_abs(a, 0)
            score_abs(a, 1)
            softplus(a, 0)
            softplus(a, 1)
            v_lo(a)
            probs_split(a, 0)
            probs_split(a, 1)
            o_lo(a)

            def residual(c, first, done_sem, done, bank_):
                dve.wait_ge(done_sem, done)
                nc.vector.tensor_tensor(X[:, c, :], RES[bank_], X[:, c, :], ALU.add).then_inc(resid_done, 1)

            def next_lo(c, before, gains):
                dve.wait_ge(hh_done, c + (before + 1))
                nc.vector.scalar_tensor_tensor(HL[:, c, :], X[:, c, :], VEC[:, bass.ds(gains + c, 1)],
                                               HH[:, c, :].bitcast(F32), ALU.mult, ALU.subtract).then_inc(hl_done, 1)

            def wo_pair(i, prepared=False):
                if not prepared:
                    lo(1, i + USE_WO)
                residual(2 * i, RES_WO, unit_done[0], i + (USE_WO + 1), 0)
                lo(0, i + (USE_WO + 1))
                next_lo(2 * i, KT, V_FFN)
                residual(2 * i + 1, RES_WO, unit_done[1], i + (USE_WO + 1), 1)
                next_lo(2 * i + 1, KT, V_FFN)

            wo_pair(0, prepared=True)
            with dve.Fori(1, KT // 2) as i:
                wo_pair(i)

            def f_lo(layer, f):
                dve.wait_ge(fh_done, f + (FT * layer + 1))
                nc.vector.tensor_tensor(FL[:, f, :], A[:], FH[:, f, :].bitcast(F32), ALU.subtract).then_inc(fl_done, 1)

            def gate_up(layer, f):
                lo(1, f + USE_GU[layer])
                if not (isinstance(f, int) and f == 0):
                    f_lo(layer, f - 1)
                if isinstance(f, int):
                    dve.wait_ge(r_ready, layer * 2 + 2)
                dve.wait_ge(unit_done[0], f + (USE_GU[layer] + 1))
                nc.vector.tensor_tensor(G[:], GATE, R[:], ALU.mult).then_inc(g_done, 1)
                lo(0, f + (USE_GU[layer] + 1))
                dve.wait_ge(unit_done[1], f + (USE_GU[layer] + 1))
                nc.vector.tensor_tensor(U[:], UP, R[:], ALU.mult).then_inc(u_done, 1)

            def ffn(layer):
                gate_up(layer, 0)
                with dve.Fori(1, FT) as f:
                    gate_up(layer, f)
                f_lo(layer, FT - 1)

                def down(c, j, last=False):
                    lo(1, c + USE_DOWN[layer])
                    lo(2, c + USE_DOWN2[layer])
                    if not last:
                        lo(0, c + (USE_DOWN[layer] + 1))
                    done = c + (USE_DOWN2[layer] + 1)
                    if layer == 0:
                        residual(c, RES_DOWN[0], unit_done[2], done, j)
                    else:
                        if not (isinstance(c, int) and c == j):
                            dve.wait_ge(stored[j], (c - j) * 8)
                        dve.wait_ge(unit_done[2], done)
                        nc.vector.tensor_tensor(Y[j][:], RES[j], X[:, c, :], ALU.add).then_inc(resid_done, 1)

                if layer == 0:
                    with dve.Fori(0, KT // 2) as i:
                        for j in range(2):
                            down(2 * i + j, j)
                else:
                    for j in range(2):
                        down(j, j)
                    with dve.Fori(1, KT // 2 - 1) as i:
                        for j in range(2):
                            down(2 * i + j, j)
                    for j in range(2):
                        down(KT - 2 + j, j, last=j == 1)

            ffn(0)
            lo(1, USE_POOL)
            dve.wait_ge(r_ready, 3)
            dve.wait_ge(padz, 5)
            for k in (KT - 2, KT - 1, *range(KT - 2)):
                nc.vector.scalar_tensor_tensor(HP[:, k, PAD:], X[:, k, :], VEC[:, V_MIX + KT + k:V_MIX + KT + k + 1],
                                               R[:], ALU.mult, ALU.mult).then_inc(hp_done, 1)
            wins = 0
            dve.wait_ge(inv_loaded, 16)
            dve.wait_ge(hp_done, KT)

            def pool_residual(g):
                for c in (2 * g, 2 * g + 1):
                    j = c % 2
                    if g < len(WINDOWS) - 1:
                        dve.wait_ge(pool_done, c + 1)
                    else:
                        dve.wait_ge(unit_done[j], USE_POOL + 1)
                    nc.vector.scalar_tensor_tensor(X[:, c, :], RES[j], VEC[:, V_SCALE + c:V_SCALE + c + 1], X[:, c, :],
                                                   ALU.mult, ALU.add).then_inc(resid_done, 1)

            for g, w in enumerate(WINDOWS):
                h = HP[:, 2 * g:2 * g + 2, :]
                src = h
                if g < len(WINDOWS) - 1:
                    for lv in range(g + 1):
                        sh = 1 << lv
                        if wins:
                            dve.wait_ge(win_done, wins)
                        nc.vector.tensor_tensor(WIN[lv % 2][:, :, PAD:], src[:, :, PAD:],
                                                src[:, :, PAD - sh:PAD + SEQ - sh], ALU.add).then_inc(win_done, 1)
                        src = WIN[lv % 2]
                        wins += 1
                else:
                    dve.wait_ge(winp_done, g + 1)
                    src = WINP[g % 2]
                dve.wait_ge(win_done, wins)
                nc.vector.scalar_tensor_tensor(PD[g % 2][:], src[:, :, PAD:], 1.0 / w, h[:, :, PAD:],
                                               ALU.mult, ALU.subtract).then_inc(win_done, 1)
                nc.vector.tensor_tensor(W16[:], src[:, :, PAD:2 * PAD], INV[:, g].to_broadcast([P, 2, PAD]), ALU.mult)\
                    .then_inc(win_done, 1)
                wins += 2
                dve.wait_ge(win_done, wins)
                nc.vector.tensor_tensor(PD[g % 2][:, :, 0:PAD], W16[:], h[:, :, PAD:2 * PAD], ALU.subtract)\
                    .then_inc(pd_done, 1)
                if g:
                    pool_residual(g - 1)
                dve.wait_ge(pdh_done, g + 1)
                nc.vector.tensor_tensor(HL[:, 2 * g:2 * g + 2, :], PD[g % 2][:], HH[:, 2 * g:2 * g + 2, :].bitcast(F32),
                                        ALU.subtract).then_inc(pdl_done, 1)
                if g:
                    for c in (2 * g - 2, 2 * g - 1):
                        next_lo(c, 2 * KT, V_FFN + KT)
            pool_residual(len(WINDOWS) - 1)
            lo(0, USE_POOL + 1)
            for c in (KT - 2, KT - 1):
                next_lo(c, 2 * KT, V_FFN + KT)
            ffn(1)

        @block.tensor
        def _(pe):
            def passes(out_, wh, wl, xh, xl, start, stop=False, check=False):
                nc.tensor.matmul(out_, wh, xh, start=start, stop=False, skip_group_check=check)
                nc.tensor.matmul(out_, wh, xl, start=False, stop=False, skip_group_check=check)
                return nc.tensor.matmul(out_, wl, xh, start=False, stop=stop, skip_group_check=check)

            def unit(slot, use, out_, xh, xl, x0=0, tiles=UK, first=True, last=True, step=None, w0=0):
                pe.wait_ge(lo_ready[slot], use + 1)
                for k in range(tiles):
                    if step is not None:
                        pe.wait_ge(hl_done, step + k + 1)
                    w = slice((w0 + k) * P, (w0 + k + 1) * P)
                    mm = passes(out_, WH[slot][:, w], WL[slot][:, w], xh[:, x0 + k, :], xl[:, x0 + k, :],
                                first and k == 0, last and k == tiles - 1)
                return mm

            pe.wait_ge(ones_ready, 1)
            pe.wait_ge(const_ready, 6)
            for k in range(KT):
                pe.wait_ge(xsq_done, k + 1)
                mm = nc.tensor.matmul(bank(0), ONES[:], XSQ[:, k, :], start=k == 0, stop=k == KT - 1)
            mm.then_inc(stats_done, 1)

            def project(n, j, step=None):
                if not (isinstance(n, int) and 3 * n + j == 0):
                    pe.wait_ge(proj_copied, 3 * n + j)
                unit(j, n, PROJ, HH, HL, step=step).then_inc(unit_done[j], 1)

            def qk_sums(n, j):
                pe.wait_ge(qksq_done, 2 * n + (j + 1))
                if not isinstance(n, int):
                    pe.wait_ge(misc_read, 4 * n + (j - 1))
                elif j:
                    pe.wait_ge(misc_read, 1)
                nc.tensor.matmul(MISC, PAIRONES[:], SQ[:], start=True, stop=True).then_inc(norm_done, 1)

            project(0, 0, step=0)
            project(0, 1)
            qk_sums(0, 0)
            project(0, 2)
            qk_sums(0, 1)
            pe.wait_ge(tri_ready, 2)
            pe.wait_ge(vzero, 2)

            def scores(a):
                pe.wait_ge(qkl_done, 2 * a + 2)
                for h in range(2):
                    hp = slice(h * HD, (h + 1) * HD)
                    for i in range(QB):
                        passes(Z[h][:, ZOFF[i]:ZOFF[i] + ZW[i]], QKH[1][hp, i * P:(i + 1) * P],
                               QKL[1][hp, i * P:(i + 1) * P], QKH[0][hp, i * P:], QKL[0][hp, i * P:],
                               start=i < 3, check=True)
                for h in range(2):
                    for i in range(QB):
                        mm = nc.tensor.matmul(Z[h][:, ZOFF[i]:ZOFF[i] + P], IDENTB[:], MASKB[:], start=False,
                                              stop=True, skip_group_check=True)
                    mm.then_inc(z_done, 1)

            def turn_v(a):
                pe.wait_ge(proj_copied, 3 * a + 3)
                pe.wait_ge(misc_read, 4 * a + 2)
                for b in range(QB):
                    mm = nc.tensor.transpose(MISC[:, b * P:(b + 1) * P], VT[:, b * P:(b + 1) * P], IDENT[:])
                mm.then_inc(vt_done, 1)

            def tails(a, h):
                pe.wait_ge(spl_done, 2 * a + (h + 1))
                for part in (AH[h], AL[h]):
                    for i in range(QB):
                        for j in range(i, QB):
                            mm = nc.tensor.matmul(Z[h][:, ZOFF[i] + (j - i) * P:ZOFF[i] + ZW[i]],
                                                  NEGTRI[:] if i == j else NEGONES[:],
                                                  part[:, ZOFF[j]:ZOFF[j] + ZW[j]],
                                                  start=False, stop=True, skip_group_check=True)
                mm.then_inc(tail_done, 1)

            def mix_values(a, read):
                pe.wait_ge(misc_read, read)
                for h in range(2):
                    pe.wait_ge(pl_done, 2 * a + (h + 1))
                    vh = VH[:, :, 2 * h:2 * h + 2, :].rearrange("p b h d -> p b (h d)")
                    vl = VL[:, :, 2 * h:2 * h + 2, :].rearrange("p b h d -> p b (h d)")
                    for i in range(QB):
                        z = slice(ZOFF[i], ZOFF[i] + ZW[i])
                        mm = passes(MISC[:, i * P:], vh[:, i, :], vl[:, i, :], AH[h][:, z], AL[h][:, z],
                                    start=h == 0 and i == 0, stop=h == 1 and i == QB - 1)
                mm.then_inc(o_done, 1)

            with pe.Fori(0, PAIRS - 1) as a:
                n = a + 1
                scores(a)
                project(n, 0)
                turn_v(a)
                project(n, 1)
                qk_sums(n, 0)
                tails(a, 0)
                tails(a, 1)
                qk_sums(n, 1)
                project(n, 2)
                mix_values(a, 4 * a + 5)
            a = PAIRS - 1
            scores(a)
            turn_v(a)
            pe.wait_ge(proj_copied, 3 * PAIRS)
            unit(0, USE_WO, RES[0], OH, OL, tiles=KT - 1, last=False)
            tails(a, 0)
            tails(a, 1)
            mix_values(a, 4 * a + 3)

            pe.wait_ge(misc_read, 4 * PAIRS)
            unit(0, USE_WO, RES[0], OH, OL, x0=KT - 1, tiles=1, first=False, w0=KT - 1).then_inc(unit_done[0], 1)
            unit(1, USE_WO, RES[1], OH, OL).then_inc(unit_done[1], 1)
            with pe.Fori(1, KT // 2) as i:
                for j in range(2):
                    pe.wait_ge(resid_done, 2 * i + (j - 1))
                    unit(j, i + USE_WO, RES[j], OH, OL).then_inc(unit_done[j], 1)

            def sum_squares():
                nc.tensor.matmul(MISC, ONES[:], SQSUM[:], start=True, stop=True).then_inc(stats_done, 1)

            def gate_up(layer, f):
                first = isinstance(f, int)
                if not (first and layer == 0):
                    pe.wait_ge(g_done, f + FT * layer)
                unit(0, f + USE_GU[layer], GATE, HH, HL, step=KT * (layer + 1) if first else None)\
                    .then_inc(unit_done[0], 1)
                if first:
                    pe.wait_ge(sqsum_done, (KT + 1) * (2 * layer + 1))
                    sum_squares()
                if not (first and layer == 0):
                    pe.wait_ge(u_done, f + FT * layer)
                unit(1, f + USE_GU[layer], UP, HH, HL).then_inc(unit_done[1], 1)

            def ffn(layer):
                gate_up(layer, 0)
                with pe.Fori(1, FT) as f:
                    gate_up(layer, f)
                with pe.Fori(0, KT // 2) as i:
                    for j in range(2):
                        c = 2 * i + j
                        pe.wait_ge(resid_done, c + (RES_DOWN[layer] - 1))
                        for u, (k0, k1) in enumerate(DOWN_UNITS):
                            pe.wait_ge(fl_done, FT * layer + k1)
                            use = c + (USE_DOWN2[layer] if u == 2 else USE_DOWN[layer])
                            unit(u, use, RES[j], FH, FL, x0=k0, tiles=k1 - k0, first=u == 0, last=u == 2)\
                                .then_inc(unit_done[u], 1)

            ffn(0)
            pe.wait_ge(sqsum_done, 2 * (KT + 1))
            sum_squares()
            for g in range(len(WINDOWS)):
                pe.wait_ge(pdl_done, g + 1)
                for j in range(2):
                    pe.wait_ge(resid_done, RES_POOL + 2 * g + j - 1)
                    mm = unit(j, USE_POOL, RES[j], HH, HL, x0=2 * g, tiles=2, w0=2 * g)
                    mm.then_inc(pool_done if g < len(WINDOWS) - 1 else unit_done[j], 1)
            ffn(1)


def kernel(x, mix_norm, ffn_norm, attn_w_qkv, attn_q_norm, attn_k_norm, attn_w_o,
           pool_w, pool_scale, ffn_w_gu, ffn_w_down):
    import concourse.bacc as bacc
    from concourse.bass_utils import run_bass_kernel_spmd

    def tiles(v):
        return np.asarray(v).reshape(-1, P).T

    arrays = {
        "x": np.asarray(x).reshape(SEQ, KT, P).transpose(2, 1, 0),
        "vectors": np.concatenate([tiles(mix_norm), tiles(ffn_norm), tiles(pool_scale),
                                   tiles([np.asarray(attn_q_norm)] * 2), tiles([np.asarray(attn_k_norm)] * 2)], 1),
        "inverse_counts": np.broadcast_to(
            np.array([[[1.0 / min(t + 1, w) for t in range(PAD)]] for w in WINDOWS], np.float32),
            (P, len(WINDOWS), 1, PAD)),
        "w_qkv": np.asarray(attn_w_qkv).reshape(KT, P, 3, PAIRS, P).transpose(3, 2, 1, 0, 4)
                   .reshape(PAIRS, 3, P, UK * P),
        "w_o": np.asarray(attn_w_o).reshape(KT, P, KT, P).transpose(2, 1, 0, 3).reshape(KT // 2, 2, P, UK * P),
        "w_gu": np.asarray(ffn_w_gu).reshape(2, KT, P, 2, FT, P).transpose(0, 4, 3, 2, 1, 5)
                  .reshape(2, FT, 2, P, UK * P),
        "w_down": np.asarray(ffn_w_down).reshape(2, FT, P, KT, P).transpose(0, 3, 2, 1, 4)
                    .reshape(2, KT, P, FT * P),
        "w_pool": np.asarray(pool_w).reshape(4, 2, P, 2, P).transpose(3, 2, 0, 1, 4).reshape(2, P, UK * P),
    }
    nc = bacc.Bacc("TRN2", target_bir_lowering=False, num_devices=1)
    args, ins = [], {}
    for name, a in arrays.items():
        ins[f"in_{name}"] = np.ascontiguousarray(a)
        args.append(nc.dram_tensor(f"in_{name}", ins[f"in_{name}"].shape, F32, kind="ExternalInput").ap())
    out = nc.dram_tensor("out_y", (P, KT, SEQ), F32, kind="ExternalOutput").ap()
    build(nc, *args, out)
    r = run_bass_kernel_spmd(nc, [ins], core_ids=[0])
    y = np.asarray(r.results[0]["out_y"])
    return y.transpose(2, 1, 0).reshape(1, SEQ, D)
```

```python
from contextlib import ExitStack

import numpy as np

import concourse.bass as bass
from concourse import mybir

F32, F32R, BF16, I32 = mybir.dt.float32, mybir.dt.float32r, mybir.dt.bfloat16, mybir.dt.int32
ALU, ACT = mybir.AluOpType, mybir.ActivationFunctionType

P = 128
D, SEQ, HEADS, HD = 1024, 512, 16, 64
DFF = 2816
EPS = 1e-6
KT = D // P
FT = DFF // P
QB = SEQ // P
PAIRS = HEADS // 2
WINDOWS = (2, 4, 8, 16)
GW = D // len(WINDOWS)
REACH = P + max(WINDOWS)
UK = 8
DOWN_UNITS = ((0, 8), (8, 16), (16, FT))
MASKED = -1e30

ZOFF = (0, 512, 1024, 896)
ZW = tuple(SEQ - P * i for i in range(QB))
ZCOLS = sum(ZW)

USE_WO = PAIRS
USE_GU = (USE_WO + KT // 2, USE_WO + KT // 2 + FT + KT + 1)
USE_DOWN = (USE_GU[0] + FT, USE_GU[1] + FT)
USE_POOL = (USE_DOWN[0] + KT - 1, USE_DOWN[0] + KT)
USE_LAST_DOWN = (USE_DOWN[0] + KT, USE_DOWN[0] + KT - 1, PAIRS + KT - 1)
USE_DOWN2 = (PAIRS, PAIRS + KT)
RES_WO, RES_DOWN, RES_POOL = 0, (KT, 3 * KT), 2 * KT
SPLIT_FFN, SPLIT_POOL = (KT, 3 * KT), 2 * KT
SUMS, SQUARES = (0, KT + 1, 2 * KT + 1), (0, KT)
V_MIX, V_FFN, V_SCALE, V_Q, V_K = 0, 2 * KT, 4 * KT, 5 * KT, 5 * KT + 1


def build(nc, x_in, vec_in, table_in, wqkv, wo, wgu, wdown, wpool, out):
    ctx = ExitStack()

    def sb(name, shape, dt=F32, where=ctx):
        return where.enter_context(nc.sbuf_tensor(name, shape, dt))

    def sem(name):
        return ctx.enter_context(nc.semaphore(name))

    with ctx:
        X = sb("X", [P, KT, SEQ])
        HH = sb("HH", [P, KT, SEQ], F32R)
        HL = sb("HL", [P, KT, SEQ], F32R)
        RAW = [sb(f"RAW{s}", [P, UK * P]) for s in range(3)]
        WH = [sb(f"WH{s}", [P, UK * P], F32R) for s in range(3)]
        WL = [sb(f"WL{s}", [P, UK * P], F32R) for s in range(3)]
        R = sb("R", [P, SEQ])
        SQ = sb("SQ", [P, SEQ])
        SQSUM = sb("SQSUM", [P, SEQ])
        VEC = sb("VEC", [P, 5 * KT + 2])
        RT = sb("RT", [P, QB, 1])
        EPSC = sb("EPSC", [P, 1])
        ONES = sb("ONES", [P, P])
        PAIRONESF = sb("PAIRONESF", [P, P])
        PAIRONES = sb("PAIRONES", [P, P], F32R)
        IDENT = sb("IDENT", [P, P])
        IDENTB = sb("IDENTB", [P, P], BF16)
        MASKB = sb("MASKB", [P, P], BF16)
        TRIF = sb("TRIF", [P, P])
        NEGTRI = sb("NEGTRI", [P, P], F32R)
        NEGONES = sb("NEGONES", [P, P], F32R)
        with ExitStack() as start:
            XSQ = sb("XSQ", [P, KT, SEQ], where=start)
        with ExitStack() as attn:
            OH = sb("OH", [P, PAIRS, SEQ], F32R, attn)
            OL = sb("OL", [P, PAIRS, SEQ], F32R, attn)
            QKF = [sb(f"{n}F", [P, SEQ], where=attn) for n in "QK"]
            QKH = [sb(f"{n}H", [P, SEQ], F32R, attn) for n in "QK"]
            QKL = [sb(f"{n}L", [P, SEQ], F32R, attn) for n in "QK"]
            VT = sb("VT", [P, SEQ], where=attn)
            VH = sb("VH", [P, QB, 4, HD], F32R, attn)
            VL = sb("VL", [P, QB, 4, HD], F32R, attn)
            RS = sb("RS", [P, SEQ], where=attn)
            SQH = sb("SQH", [P, SEQ], F32R, attn)
            SQL = sb("SQL", [P, SEQ], F32R, attn)
            E = [sb(f"E{h}", [P, ZCOLS], where=attn) for h in range(2)]
            SP = [sb(f"SP{h}", [P, ZCOLS], where=attn) for h in range(2)]
            AH = [sb(f"AH{h}", [P, ZCOLS], F32R, attn) for h in range(2)]
            AL = [sb(f"AL{h}", [P, ZCOLS], F32R, attn) for h in range(2)]
        FIRST_SQ = [(SQ[:], SQH[:], SQL[:]), (E[0][:, 0:SEQ], AH[0][:, 0:SEQ], AL[0][:, 0:SEQ])]
        with ExitStack() as ffn:
            FH = sb("FH", [P, FT, SEQ], F32R, ffn)
            FL = sb("FL", [P, FT, SEQ], F32R, ffn)
            G = sb("G", [P, SEQ], where=ffn)
            S = sb("S", [P, SEQ], where=ffn)
            U = sb("U", [P, SEQ], where=ffn)
            A = sb("A", [P, SEQ], where=ffn)
        Y = [G, S]
        with ExitStack() as pool_mix:
            sb("FH_FIRST", [P, 2 * KT, SEQ], F32R, pool_mix)
            BAND = sb("BAND", [P, len(WINDOWS), QB, REACH], where=pool_mix)
            sb("FH_REST", [P, (FT - 2 * KT) * SEQ - len(WINDOWS) * QB * REACH], where=pool_mix)
            sb("FL_FIRST", [P, 2 * KT, SEQ], F32R, pool_mix)
            XSQ2 = sb("XSQ2", [P, QB, SEQ], where=pool_mix)
            sb("FL_REST", [P, FT - 2 * KT - QB, SEQ], where=pool_mix)
            TABLE = sb("TABLE", [P, len(WINDOWS), 2, REACH], where=pool_mix)
        UH = FH[:, KT:2 * KT, :].rearrange("p (g x) s -> p g (x s)", x=2)
        UL = FL[:, KT:2 * KT, :].rearrange("p (g x) s -> p g (x s)", x=2)

        def bands(tiles):
            flat = tiles.rearrange("p f s -> p (f s)")[:, 0:len(WINDOWS) * QB * REACH]
            return flat.rearrange("p (g b c) -> p g b c", g=len(WINDOWS), b=QB)

        BANDH, BANDL = bands(FH[:, 0:5, :]), bands(FL[:, 0:5, :])

        PS = ctx.enter_context(nc.psum_tensor("PS", [P, 8 * 512], F32))

        def bank(b, n=1):
            return PS[:, b * 512:(b + n) * 512]

        def ref_order(row):
            return row.rearrange("p (r b) -> p b r", b=QB)

        def by_block(row):
            return row.rearrange("p (b r) -> p b r", b=QB)

        Z = [bank(0, 3)[:, 0:ZCOLS], bank(3, 3)[:, 0:ZCOLS]]
        PROJ, MISC = bank(6), bank(7)
        RES = [bank(6), bank(7)]
        TOK = [bank(0, 2), bank(2, 2), bank(4, 2), bank(0, 2)]
        POOLED = [bank(b) for b in (6, 7, 2, 3, 4, 5, 6, 7)]
        GATE, UP = bank(0), bank(1)
        FIRST_SUMS = (bank(1), bank(2))

        x_loaded = [sem(f"x_loaded{i}") for i in range(4)]
        vec_loaded, table_loaded = sem("vec_loaded"), sem("table_loaded")
        raw_full = [sem(f"raw_full{s}") for s in range(3)]
        hi_ready = [sem(f"hi_ready{s}") for s in range(3)]
        lo_ready = [sem(f"lo_ready{s}") for s in range(3)]
        unit_done = [sem(f"unit_done{s}") for s in range(3)]
        stored = [sem(f"stored{i}") for i in range(2)]
        made, const_ready, tri_ready, vzero = sem("made"), sem("const_ready"), sem("tri_ready"), sem("vzero")
        eps_ready, gain_ready, ones_ready = sem("eps_ready"), sem("gain_ready"), sem("ones_ready")
        xsq_done, xsq_even, stats_done, ln_done, r_ready = sem("xsq_done"), sem("xsq_even"), sem("stats_done"), sem("ln_done"), sem("r_ready")
        hh_done, hl_done, xsum_done = sem("hh_done"), sem("hl_done"), sem("xsum_done")
        sq_one, sqsum_done = sem("sq_one"), sem("sqsum_done")
        resid_done = sem("resid_done")
        qksq_done, qksh_done, qksl_done, norm_done = sem("qksq_done"), sem("qksh_done"), sem("qksl_done"), sem("norm_done")
        rs_done, qkn_done, qkh_done, qkl_done = sem("rs_done"), sem("qkn_done"), sem("qkh_done"), sem("qkl_done")
        proj_read, misc_read = sem("proj_read"), sem("misc_read")
        vt_done, vh_done = sem("vt_done"), sem("vh_done")
        z_done, abs_done, exp_done, l_done = sem("z_done"), sem("abs_done"), sem("exp_done"), sem("l_done")
        sp_done, sph_done, spl_done, tail_done = sem("sp_done"), sem("sph_done"), sem("spl_done"), sem("tail_done")
        prob_done, ph_done, pl_done = sem("prob_done"), sem("ph_done"), sem("pl_done")
        o_done, oh_done = sem("o_done"), sem("oh_done")
        g_done, s_done, u_done, a_done = sem("g_done"), sem("s_done"), sem("u_done"), sem("a_done")
        fh_done, fl_done = sem("fh_done"), sem("fl_done")
        tok_done, uh_done, ul_done, last_sq = sem("tok_done"), sem("uh_done"), sem("ul_done"), sem("last_sq")
        band_done, bandh_done, bandl_done = sem("band_done"), sem("bandh_done"), sem("bandl_done")
        pool_done = sem("pool_done")

        block = ctx.enter_context(nc.Block())

        @block.sync
        def _(sp):
            def load(slot, use, src, tiles=UK):
                if not (isinstance(use, int) and use == 0):
                    sp.wait_ge(lo_ready[slot], use)
                sp.dma_start(RAW[slot][:, 0:tiles * P], src).then_inc(raw_full[slot], 16)

            sp.dma_start(VEC[:], vec_in).then_inc(vec_loaded, 16)
            for i in range(4):
                sp.dma_start(X[:, 2 * i:2 * i + 2, :], x_in[:, 2 * i:2 * i + 2, :]).then_inc(x_loaded[i], 16)
                if i == 0:
                    load(0, 0, wqkv[0, 0])
            for j in range(1, 3):
                load(j, 0, wqkv[0, j])
            with sp.Fori(1, PAIRS) as n:
                for j in range(3):
                    load(j, n, wqkv[n, j])
            with sp.Fori(0, KT // 2) as i:
                for j in range(2):
                    load(j, i + USE_WO, wo[i, j])
            for layer in range(2):
                with sp.Fori(0, FT) as f:
                    for j in range(2):
                        load(j, f + USE_GU[layer], wgu[layer, f, j])

                def down(c, order=(0, 1, 2)):
                    for j in order:
                        k0, k1 = DOWN_UNITS[j]
                        use = c + (USE_DOWN2[layer] if j == 2 else USE_DOWN[layer])
                        if layer == 0 and isinstance(c, int):
                            use = USE_LAST_DOWN[j]
                        load(j, use, wdown[layer, c, :, k0 * P:k1 * P], k1 - k0)

                with sp.Fori(0, KT - 1) as c:
                    down(c)
                if layer == 0:
                    load(0, USE_POOL[0], wpool[0])
                    sp.wait_ge(a_done, FT)
                    sp.dma_start(TABLE[:], table_in).then_inc(table_loaded, 16)
                    down(KT - 1, (1, 2, 0))
                    load(1, USE_POOL[1], wpool[1])
                else:
                    down(KT - 1)

        @block.gpsimd
        def _(pool):
            nc.gpsimd.memset(IDENT[:], 0.0).then_inc(made, 1)
            nc.gpsimd.memset(IDENTB[:], 0.0).then_inc(made, 1)
            nc.gpsimd.memset(MASKB[:], MASKED).then_inc(made, 1)
            nc.gpsimd.memset(TRIF[:], -1.0).then_inc(made, 1)
            nc.gpsimd.memset(PAIRONESF[:], 0.0).then_inc(made, 1)
            pool.wait_ge(made, 5)
            for t in (IDENT, IDENTB):
                nc.gpsimd.affine_select(out=t[:], in_=t[:], compare_op=ALU.not_equal, fill=1.0, base=0,
                                        pattern=[[-1, P]], channel_multiplier=1).then_inc(const_ready, 1)
            nc.gpsimd.affine_select(out=MASKB[:], in_=MASKB[:], compare_op=ALU.is_ge, fill=0.0, base=0,
                                    pattern=[[-1, P]], channel_multiplier=1).then_inc(const_ready, 1)
            nc.gpsimd.affine_select(out=TRIF[:], in_=TRIF[:], compare_op=ALU.is_ge, fill=0.0, base=0,
                                    pattern=[[-1, P]], channel_multiplier=1).then_inc(const_ready, 1)
            for h in range(2):
                pool.wait_ge(const_ready, 4 + h)
                nc.gpsimd.memset(PAIRONESF[h * HD:(h + 1) * HD, h * HD:(h + 1) * HD], 1.0).then_inc(const_ready, 1)
            for k in range(0, KT, 2):
                pool.wait_ge(const_ready, 6)
                pool.wait_ge(x_loaded[k // 2], 16)
                nc.gpsimd.tensor_tensor(XSQ[:, k, :], X[:, k, :], X[:, k, :], ALU.mult).then_inc(xsq_even, 1)
            nc.gpsimd.memset(VH[:].bitcast(F32), 0.0).then_inc(vzero, 1)
            nc.gpsimd.memset(VL[:].bitcast(F32), 0.0).then_inc(vzero, 1)

            def qk_square(n, j):
                if j == 0:
                    pool.wait_ge(proj_read, 3 * n + 1)
                else:
                    pool.wait_ge(misc_read, 4 * n)
                pool.wait_ge(qksl_done, 2 * n + j)
                nc.gpsimd.tensor_tensor(SQ[:], QKF[j][:], QKF[j][:], ALU.mult).then_inc(qksq_done, 1)
                pool.wait_ge(norm_done, 2 * n + j)
                pool.wait_ge(qksq_done, 2 * n + (j + 1))
                nc.gpsimd.tensor_tensor(SQH[:], QKF[j][:], QKF[j][:], ALU.mult).then_inc(qksh_done, 1)
                pool.wait_ge(qksh_done, 2 * n + (j + 1))
                nc.gpsimd.tensor_tensor(SQL[:], SQ[:], SQH[:].bitcast(F32), ALU.subtract).then_inc(qksl_done, 1)

            def qk_lo(n, j):
                pool.wait_ge(qkh_done, 2 * n + (j + 1))
                nc.gpsimd.tensor_tensor(QKL[j][:], QKF[j][:], QKH[j][:].bitcast(F32), ALU.subtract)\
                    .then_inc(qkl_done, 1)

            with pool.Fori(1, PAIRS) as n:
                qk_square(n, 0)
                qk_square(n, 1)
                qk_lo(n, 0)
                qk_lo(n, 1)

            def square_sum(round_, first, tiles):
                pool.wait_ge(stats_done, round_ + 1)
                if round_ == 0:
                    pool.wait_ge(qksl_done, 2 * PAIRS)
                nc.gpsimd.memset(SQSUM[:], 0.0).then_inc(sqsum_done, 1)
                with pool.Fori(0, tiles) as c:
                    pool.wait_ge(sqsum_done, c + (SUMS[round_] + 1))
                    pool.wait_ge(resid_done, c + (first + 1))
                    pool.wait_ge(vec_loaded, 16)
                    nc.gpsimd.tensor_tensor(SQ[:], X[:, c, :], X[:, c, :], ALU.mult).then_inc(sq_one, 1)
                    pool.wait_ge(sq_one, c + (SQUARES[round_] + 1))
                    nc.gpsimd.tensor_tensor(SQSUM[:], SQSUM[:], SQ[:], ALU.add).then_inc(sqsum_done, 1)

            def ffn_mul(layer):
                with pool.Fori(0, FT) as f:
                    pool.wait_ge(s_done, f + (FT * layer + 1))
                    pool.wait_ge(u_done, f + (FT * layer + 1))
                    nc.gpsimd.tensor_tensor(A[:], U[:], S[:], ALU.mult).then_inc(a_done, 1)

            square_sum(0, RES_WO, KT)
            ffn_mul(0)
            square_sum(1, RES_DOWN[0], KT - 1)
            pool.wait_ge(r_ready, 3)
            pool.wait_ge(unit_done[2], USE_LAST_DOWN[2] + 1)
            pool.wait_ge(table_loaded, 16)
            for g in range(len(WINDOWS)):
                nc.gpsimd.tensor_tensor(BAND[:, g, 0:1, :], TABLE[:, g, 0:1, :], RT[:, 0:1, :].to_broadcast([P, 1, REACH]),
                                        ALU.mult).then_inc(band_done, 1)
                nc.gpsimd.tensor_tensor(BAND[:, g, 1:QB, :], TABLE[:, g, 1:2, :].to_broadcast([P, QB - 1, REACH]),
                                        RT[:, 1:QB, :].to_broadcast([P, QB - 1, REACH]), ALU.mult)\
                    .then_inc(band_done, 1)
            pool.wait_ge(stats_done, 3)
            for c in range(1, KT):
                pool.wait_ge(xsq_done, KT // 2 + c + 1)
                if c > 1:
                    pool.wait_ge(sqsum_done, SUMS[2] + c - 1)
                nc.gpsimd.tensor_tensor(SQSUM[:], XSQ2[:, 0, :] if c == 1 else SQSUM[:], XSQ2[:, c % QB, :], ALU.add)\
                    .then_inc(sqsum_done, 1)
            ffn_mul(1)

        @block.scalar
        def _(act):
            def hi(slot, use):
                act.wait_ge(raw_full[slot], 16 * use + 16)
                if not (isinstance(use, int) and use == 0):
                    act.wait_ge(unit_done[slot], use)
                nc.scalar.activation(WH[slot][:], RAW[slot][:], ACT.Copy).then_inc(hi_ready[slot], 1)

            def inverse_rms(src, n, round_, to=R[:]):
                act.wait_ge(stats_done, round_ + 1)
                nc.scalar.activation(to, src, ACT.Ln, bias=EPSC[:], scale=1.0 / n).then_inc(ln_done, 1)
                act.wait_ge(ln_done, round_ + 1)
                nc.scalar.activation(to, to, ACT.Exp, scale=-0.5).then_inc(r_ready, 1)

            nc.scalar.preload_act_table_set("natural_log_exp_and_others")
            act.wait_ge(eps_ready, 1)
            def start_square(k):
                nc.scalar.activation(XSQ[:, k, :], X[:, k, :], ACT.Square).then_inc(xsq_done, 1)

            act.wait_ge(vec_loaded, 16)
            for i in range(KT // 2):
                act.wait_ge(x_loaded[i], 16)
                for k in (2 * i, 2 * i + 1):
                    nc.scalar.activation(HH[:, k, :], X[:, k, :], ACT.Copy, scale=VEC[:, V_MIX + k:V_MIX + k + 1])\
                        .then_inc(hh_done, 1)
                if i == 0:
                    hi(0, 0)
                else:
                    start_square(2 * i - 1)
            start_square(KT - 1)
            hi(1, 0)
            act.wait_ge(const_ready, 6)
            nc.scalar.activation(NEGTRI[:], TRIF[:], ACT.Copy).then_inc(tri_ready, 1)
            nc.scalar.activation(PAIRONES[:], PAIRONESF[:], ACT.Copy).then_inc(tri_ready, 1)
            hi(2, 0)
            inverse_rms(bank(0), D, 0)

            def qk_rms(n, j, sums=(PROJ, MISC)):
                act.wait_ge(norm_done, 2 * n + (j + 1))
                if not (isinstance(n, int) and 2 * n + j == 0):
                    act.wait_ge(qkn_done, 2 * n + j)
                if j == 0:
                    nc.scalar.activation(RS[:], sums[0], ACT.Ln, bias=EPSC[:], scale=1.0 / HD).then_inc(proj_read, 1)
                    act.wait_ge(proj_read, 3 * n + 2)
                else:
                    nc.scalar.activation(RS[:], sums[1], ACT.Ln, bias=EPSC[:], scale=1.0 / HD).then_inc(misc_read, 1)
                    act.wait_ge(misc_read, 2 if isinstance(n, int) else 4 * n + 1)
                nc.scalar.activation(RS[:], RS[:], ACT.Exp, scale=-0.5).then_inc(rs_done, 1)

            def qk_hi(n, j):
                act.wait_ge(qkn_done, 2 * n + (j + 1))
                nc.scalar.activation(QKH[j][:], QKF[j][:], ACT.Copy).then_inc(qkh_done, 1)

            for j in range(2):
                act.wait_ge((proj_read, misc_read)[j], 1)
                nc.scalar.activation(FIRST_SQ[j][0], QKF[j][:], ACT.Square).then_inc(qksq_done, 1)
                nc.scalar.activation(FIRST_SQ[j][1], QKF[j][:], ACT.Square).then_inc(qksh_done, 1)
            for j in range(2):
                qk_rms(0, j, FIRST_SUMS)
                qk_hi(0, j)
            hi(0, 1)

            def score_exp(a, h):
                act.wait_ge(abs_done, 2 * a + (h + 1))
                nc.scalar.activation(E[h][:], E[h][:], ACT.Exp, scale=-1.0).then_inc(exp_done, 1)

            def score_ln(a, h):
                act.wait_ge(exp_done, 2 * a + (h + 1))
                nc.scalar.activation(E[h][:], E[h][:], ACT.Ln, bias=1.0).then_inc(l_done, 1)

            def v_hi(a):
                act.wait_ge(vt_done, a + 1)
                nc.scalar.activation(VH[:, :, 0:4:3, :], MISC.rearrange("p (b h d) -> p b h d", b=QB, h=2),
                                     ACT.Copy).then_inc(vh_done, 1)

            def probs(a, h):
                act.wait_ge(tail_done, 2 * a + (h + 1))
                nc.scalar.activation(E[h][:], Z[h], ACT.Exp).then_inc(prob_done, 1)

            def o_hi(a):
                act.wait_ge(o_done, a + 1)
                act.wait_ge(vec_loaded, 16)
                nc.scalar.activation(ref_order(OH[:, a, :]), by_block(MISC), ACT.Copy).then_inc(oh_done, 1)

            with act.Fori(0, PAIRS - 1) as a:
                n = a + 1
                hi(1, n)
                score_exp(a, 0)
                v_hi(a)
                score_ln(a, 0)
                score_exp(a, 1)
                score_ln(a, 1)
                hi(2, n)
                hi(0, n + 1)
                probs(a, 0)
                qk_rms(n, 0)
                qk_hi(n, 0)
                probs(a, 1)
                qk_rms(n, 1)
                qk_hi(n, 1)
                o_hi(a)
            a = PAIRS - 1
            hi(1, USE_WO)
            score_exp(a, 0)
            v_hi(a)
            score_ln(a, 0)
            score_exp(a, 1)
            score_ln(a, 1)
            probs(a, 0)
            probs(a, 1)
            o_hi(a)

            def next_hi(c, first, gains):
                act.wait_ge(resid_done, c + (first + 1))
                act.wait_ge(vec_loaded, 16)
                nc.scalar.activation(HH[:, c, :], X[:, c, :], ACT.Copy, scale=VEC[:, bass.ds(gains + c, 1)])\
                    .then_inc(hh_done, 1)

            def wo_pair(i, prepared=False):
                if not prepared:
                    hi(1, i + USE_WO)
                hi(0, i + (USE_WO + 1))
                next_hi(2 * i, RES_WO, V_FFN)
                next_hi(2 * i + 1, RES_WO, V_FFN)

            wo_pair(0, prepared=True)
            with act.Fori(1, KT // 2) as i:
                wo_pair(i)

            def f_hi(layer, f):
                act.wait_ge(a_done, f + (FT * layer + 1))
                act.wait_ge(vec_loaded, 16)
                nc.scalar.activation(FH[:, f, :], A[:], ACT.Copy).then_inc(fh_done, 1)

            def gate_up(layer, f):
                hi(1, f + USE_GU[layer])
                if not (isinstance(f, int) and f == 0):
                    f_hi(layer, f - 1)
                if isinstance(f, int):
                    inverse_rms(MISC, D, layer * 2 + 1)
                act.wait_ge(g_done, f + (FT * layer + 1))
                nc.scalar.activation(S[:], G[:], ACT.Silu).then_inc(s_done, 1)
                hi(0, f + (USE_GU[layer] + 1))

            def ffn(layer):
                gate_up(layer, 0)
                with act.Fori(1, FT) as f:
                    gate_up(layer, f)
                f_hi(layer, FT - 1)

                def down(c, last=False):
                    hi(1, c + USE_DOWN[layer])
                    hi(2, c + USE_DOWN2[layer])
                    if not last:
                        hi(0, c + (USE_DOWN[layer] + 1))

                def store(c, j):
                    act.wait_ge(resid_done, c + (RES_DOWN[1] + 1))
                    act.dma_start(out[:, c, :], Y[j][:]).then_inc(stored[j], 16)

                if layer == 0:
                    with act.Fori(0, KT - 2) as c:
                        down(c)
                        next_hi(c, RES_DOWN[0], V_MIX + KT)
                else:
                    with act.Fori(0, KT // 2 - 1) as i:
                        for j in range(2):
                            down(2 * i + j)
                            store(2 * i + j, j)
                    for j in range(2):
                        down(KT - 2 + j, last=j == 1)
                        store(KT - 2 + j, j)
                    for j in range(2):
                        act.wait_ge(stored[j], 16 * (KT // 2))

            ffn(0)
            hi(1, USE_DOWN[0] + KT - 2)
            hi(2, USE_DOWN2[0] + KT - 2)
            hi(0, USE_POOL[0])
            next_hi(KT - 2, RES_DOWN[0], V_MIX + KT)
            hi(1, USE_LAST_DOWN[1])
            hi(2, USE_LAST_DOWN[2])
            hi(0, USE_LAST_DOWN[0])
            hi(1, USE_POOL[1])
            nc.scalar.preload_act_table_set("natural_log_exp_and_others")

            def token_hi(g):
                if g % 2:
                    act.wait_ge(unit_done[g // 2], USE_POOL[g // 2] + 1)
                else:
                    act.wait_ge(tok_done, g // 2 + 1)
                act.wait_ge(unit_done[1], USE_LAST_DOWN[1] + 1)
                nc.scalar.activation(UH[:, g, :], TOK[g], ACT.Copy).then_inc(uh_done, 1)

            def band_hi(g):
                act.wait_ge(band_done, 2 * g + 2)
                act.wait_ge(unit_done[0], USE_LAST_DOWN[0] + 1)
                nc.scalar.activation(BANDH[:, g], BAND[:, g], ACT.Copy).then_inc(bandh_done, 1)

            def pool_square(c):
                if c >= QB:
                    act.wait_ge(sqsum_done, SUMS[2] + c - QB + (c == QB))
                nc.scalar.activation(XSQ2[:, c % QB, :], X[:, c, :], ACT.Square).then_inc(xsq_done, 1)

            token_hi(0)
            token_hi(1)
            act.wait_ge(resid_done, 2 * KT)
            nc.scalar.activation(A[:], X[:, KT - 1, :], ACT.Square).then_inc(last_sq, 1)
            next_hi(KT - 1, RES_DOWN[0], V_MIX + KT)
            hi(0, USE_GU[1])
            inverse_rms(MISC[:, 0:QB], D, 2, RT[:, :, 0])
            band_hi(0)
            token_hi(2)
            band_hi(1)
            token_hi(3)
            band_hi(2)
            next_hi(0, RES_POOL, V_FFN + KT)
            band_hi(3)
            pool_square(0)
            for c in range(1, KT):
                next_hi(c, RES_POOL, V_FFN + KT)
                pool_square(c)
            ffn(1)

        @block.vector
        def _(dve):
            def lo(slot, use):
                dve.wait_ge(hi_ready[slot], use + 1)
                nc.vector.tensor_tensor(WL[slot][:], RAW[slot][:], WH[slot][:].bitcast(F32), ALU.subtract)\
                    .then_inc(lo_ready[slot], 1)

            nc.vector.memset(EPSC[:], EPS).then_inc(eps_ready, 1)
            nc.vector.memset(ONES[:], 1.0).then_inc(ones_ready, 1)
            nc.vector.memset(NEGONES[:].bitcast(F32), -1.0).then_inc(tri_ready, 1)
            dve.wait_ge(vec_loaded, 16)

            def add_square(k):
                dve.wait_ge(xsq_done, (k + 1) // 2)
                dve.wait_ge(xsq_even, k // 2 + 1)
                if k > 1:
                    dve.wait_ge(xsum_done, k - 1)
                nc.vector.tensor_tensor(SQSUM[:], XSQ[:, 0, :] if k == 1 else SQSUM[:], XSQ[:, k, :], ALU.add)\
                    .then_inc(xsum_done, 1)

            nc.vector.tensor_scalar(VEC[:, V_Q:V_Q + 1], VEC[:, V_Q:V_Q + 1], HD ** -0.5, None, ALU.mult)\
                .then_inc(gain_ready, 1)
            for k in range(KT):
                dve.wait_ge(hh_done, k + 1)
                nc.vector.scalar_tensor_tensor(HL[:, k, :], X[:, k, :], VEC[:, V_MIX + k:V_MIX + k + 1],
                                               HH[:, k, :].bitcast(F32), ALU.mult, ALU.subtract).then_inc(hl_done, 1)
                if k == 1:
                    lo(0, 0)
                if k >= 5:
                    add_square(k - 4)
            lo(1, 0)
            for k in range(KT - 4, KT):
                add_square(k)
            lo(2, 0)

            def scale_qk(n, j):
                dve.wait_ge(unit_done[j], n + 1)
                if isinstance(n, int):
                    dve.wait_ge(r_ready, 1)
                else:
                    dve.wait_ge(qkl_done, 2 * n + (j - 1))
                nc.vector.tensor_tensor(QKF[j][:], (PROJ, MISC)[j], R[:], ALU.mult)\
                    .then_inc((proj_read, misc_read)[j], 1)

            def scale_v(n):
                dve.wait_ge(unit_done[2], n + 1)
                nc.vector.tensor_tensor(VT[:], PROJ, R[:], ALU.mult).then_inc(proj_read, 1)

            def qk_norm(n, j):
                dve.wait_ge(rs_done, 2 * n + (j + 1))
                dve.wait_ge(gain_ready, 1)
                nc.vector.scalar_tensor_tensor(QKF[j][:], QKF[j][:], VEC[:, V_Q + j:V_Q + j + 1], RS[:],
                                               ALU.mult, ALU.mult).then_inc(qkn_done, 1)

            def first_lo(j):
                whole, hi_, lo_ = FIRST_SQ[j]
                dve.wait_ge(qksh_done, j + 1)
                nc.vector.tensor_tensor(lo_, whole, hi_.bitcast(F32), ALU.subtract).then_inc(qksl_done, 1)

            def first_qk_lo(j):
                dve.wait_ge(qkh_done, j + 1)
                nc.vector.tensor_tensor(QKL[j][:], QKF[j][:], QKH[j][:].bitcast(F32), ALU.subtract)\
                    .then_inc(qkl_done, 1)

            scale_qk(0, 0)
            scale_qk(0, 1)
            first_lo(0)
            first_lo(1)
            qk_norm(0, 0)
            first_qk_lo(0)
            qk_norm(0, 1)
            first_qk_lo(1)
            scale_v(0)
            lo(0, 1)

            def score_abs(a, h):
                dve.wait_ge(z_done, 2 * a + (h + 1))
                nc.vector.tensor_scalar(E[h][:].bitcast(I32), Z[h].bitcast(I32), 0x7FFFFFFF, None, ALU.bitwise_and)\
                    .then_inc(abs_done, 1)

            def softplus(a, h):
                dve.wait_ge(l_done, 2 * a + (h + 1))
                nc.vector.scalar_tensor_tensor(SP[h][:], Z[h], 0.0, E[h][:], ALU.max, ALU.add).then_inc(sp_done, 1)
                dve.wait_ge(sp_done, 2 * a + (h + 1))
                nc.vector.tensor_copy(AH[h][:], SP[h][:]).then_inc(sph_done, 1)
                dve.wait_ge(sph_done, 2 * a + (h + 1))
                nc.vector.tensor_tensor(AL[h][:], SP[h][:], AH[h][:].bitcast(F32), ALU.subtract).then_inc(spl_done, 1)

            def v_lo(a):
                dve.wait_ge(vh_done, a + 1)
                nc.vector.tensor_tensor(VL[:, :, 0:4:3, :], MISC.rearrange("p (b h d) -> p b h d", b=QB, h=2),
                                        VH[:, :, 0:4:3, :].bitcast(F32), ALU.subtract).then_inc(misc_read, 1)

            def probs_split(a, h):
                dve.wait_ge(prob_done, 2 * a + (h + 1))
                nc.vector.tensor_copy(AH[h][:], E[h][:]).then_inc(ph_done, 1)
                dve.wait_ge(ph_done, 2 * a + (h + 1))
                nc.vector.tensor_tensor(AL[h][:], E[h][:], AH[h][:].bitcast(F32), ALU.subtract).then_inc(pl_done, 1)

            def o_lo(a):
                dve.wait_ge(oh_done, a + 1)
                nc.vector.tensor_tensor(ref_order(OL[:, a, :]), by_block(MISC), ref_order(OH[:, a, :].bitcast(F32)),
                                        ALU.subtract)\
                    .then_inc(misc_read, 1)

            with dve.Fori(0, PAIRS - 1) as a:
                n = a + 1
                lo(1, n)
                score_abs(a, 0)
                score_abs(a, 1)
                v_lo(a)
                softplus(a, 0)
                scale_qk(n, 0)
                softplus(a, 1)
                scale_qk(n, 1)
                lo(2, n)
                lo(0, n + 1)
                probs_split(a, 0)
                qk_norm(n, 0)
                probs_split(a, 1)
                qk_norm(n, 1)
                scale_v(n)
                o_lo(a)
            a = PAIRS - 1
            lo(1, USE_WO)
            score_abs(a, 0)
            score_abs(a, 1)
            v_lo(a)
            softplus(a, 0)
            softplus(a, 1)
            probs_split(a, 0)
            probs_split(a, 1)
            o_lo(a)

            def residual(c, first, done_sem, done, bank_):
                dve.wait_ge(done_sem, done)
                nc.vector.tensor_tensor(X[:, c, :], RES[bank_], X[:, c, :], ALU.add).then_inc(resid_done, 1)

            def next_lo(c, before, gains):
                dve.wait_ge(hh_done, c + (before + 1))
                nc.vector.scalar_tensor_tensor(HL[:, c, :], X[:, c, :], VEC[:, bass.ds(gains + c, 1)],
                                               HH[:, c, :].bitcast(F32), ALU.mult, ALU.subtract).then_inc(hl_done, 1)

            def wo_pair(i, prepared=False):
                if not prepared:
                    lo(1, i + USE_WO)
                residual(2 * i, RES_WO, unit_done[0], i + (USE_WO + 1), 0)
                lo(0, i + (USE_WO + 1))
                next_lo(2 * i, SPLIT_FFN[0], V_FFN)
                residual(2 * i + 1, RES_WO, unit_done[1], i + (USE_WO + 1), 1)
                next_lo(2 * i + 1, SPLIT_FFN[0], V_FFN)

            wo_pair(0, prepared=True)
            with dve.Fori(1, KT // 2) as i:
                wo_pair(i)

            def f_lo(layer, f):
                dve.wait_ge(fh_done, f + (FT * layer + 1))
                nc.vector.tensor_tensor(FL[:, f, :], A[:], FH[:, f, :].bitcast(F32), ALU.subtract).then_inc(fl_done, 1)

            def gate_up(layer, f):
                lo(1, f + USE_GU[layer])
                if not (isinstance(f, int) and f == 0):
                    f_lo(layer, f - 1)
                if isinstance(f, int):
                    dve.wait_ge(r_ready, layer * 2 + 2)
                dve.wait_ge(unit_done[0], f + (USE_GU[layer] + 1))
                nc.vector.tensor_tensor(G[:], GATE, R[:], ALU.mult).then_inc(g_done, 1)
                lo(0, f + (USE_GU[layer] + 1))
                dve.wait_ge(unit_done[1], f + (USE_GU[layer] + 1))
                nc.vector.tensor_tensor(U[:], UP, R[:], ALU.mult).then_inc(u_done, 1)

            def ffn(layer):
                gate_up(layer, 0)
                with dve.Fori(1, FT) as f:
                    gate_up(layer, f)
                f_lo(layer, FT - 1)

                def down(c, j, last=False):
                    lo(1, c + USE_DOWN[layer])
                    lo(2, c + USE_DOWN2[layer])
                    if not last:
                        lo(0, c + (USE_DOWN[layer] + 1))
                    done = c + (USE_DOWN2[layer] + 1)
                    if layer == 0:
                        residual(c, RES_DOWN[0], unit_done[2], done, j)
                        next_lo(c, SPLIT_POOL, V_MIX + KT)
                    else:
                        if not (isinstance(c, int) and c == j):
                            dve.wait_ge(stored[j], (c - j) * 8)
                        dve.wait_ge(unit_done[2], done)
                        nc.vector.tensor_tensor(Y[j][:], RES[j], X[:, c, :], ALU.add).then_inc(resid_done, 1)

                if layer == 0:
                    with dve.Fori(0, KT // 2 - 1) as i:
                        for j in range(2):
                            down(2 * i + j, j)
                else:
                    for j in range(2):
                        down(j, j)
                    with dve.Fori(1, KT // 2 - 1) as i:
                        for j in range(2):
                            down(2 * i + j, j)
                    for j in range(2):
                        down(KT - 2 + j, j, last=j == 1)

            ffn(0)
            lo(1, USE_DOWN[0] + KT - 2)
            lo(2, USE_DOWN2[0] + KT - 2)
            lo(0, USE_POOL[0])
            residual(KT - 2, RES_DOWN[0], unit_done[2], USE_DOWN2[0] + KT - 1, 0)
            next_lo(KT - 2, SPLIT_POOL, V_MIX + KT)
            lo(1, USE_LAST_DOWN[1])
            lo(2, USE_LAST_DOWN[2])
            lo(0, USE_LAST_DOWN[0])
            lo(1, USE_POOL[1])

            def token_lo(g):
                dve.wait_ge(uh_done, g + 1)
                nc.vector.tensor_tensor(UL[:, g, :], TOK[g], UH[:, g, :].bitcast(F32), ALU.subtract)\
                    .then_inc(ul_done, 1)

            def band_lo(g):
                dve.wait_ge(bandh_done, g + 1)
                nc.vector.tensor_tensor(BANDL[:, g], BAND[:, g], BANDH[:, g].bitcast(F32), ALU.subtract)\
                    .then_inc(bandl_done, 1)

            def pool_residual(c):
                dve.wait_ge(pool_done, c + 1)
                nc.vector.scalar_tensor_tensor(X[:, c, :], POOLED[c], VEC[:, V_SCALE + c:V_SCALE + c + 1], X[:, c, :],
                                               ALU.mult, ALU.add).then_inc(resid_done, 1)

            token_lo(0)
            token_lo(1)
            residual(KT - 1, RES_DOWN[0], unit_done[0], USE_LAST_DOWN[0] + 1, 1)
            next_lo(KT - 1, SPLIT_POOL, V_MIX + KT)
            lo(0, USE_GU[1])
            band_lo(0)
            token_lo(2)
            band_lo(1)
            pool_residual(0)
            token_lo(3)
            band_lo(2)
            pool_residual(1)
            next_lo(0, SPLIT_FFN[1], V_FFN + KT)
            band_lo(3)
            for c in range(2, KT):
                pool_residual(c)
                next_lo(c - 1, SPLIT_FFN[1], V_FFN + KT)
            next_lo(KT - 1, SPLIT_FFN[1], V_FFN + KT)
            ffn(1)

        @block.tensor
        def _(pe):
            def passes(out_, wh, wl, xh, xl, start, stop=False, check=False):
                nc.tensor.matmul(out_, wh, xh, start=start, stop=False, skip_group_check=check)
                nc.tensor.matmul(out_, wh, xl, start=False, stop=False, skip_group_check=check)
                return nc.tensor.matmul(out_, wl, xh, start=False, stop=stop, skip_group_check=check)

            def unit(slot, use, out_, xh, xl, x0=0, tiles=UK, first=True, last=True, step=None, w0=0):
                pe.wait_ge(lo_ready[slot], use + 1)
                for k in range(tiles):
                    if step is not None:
                        pe.wait_ge(hl_done, step + k + 1)
                    w = slice((w0 + k) * P, (w0 + k + 1) * P)
                    mm = passes(out_, WH[slot][:, w], WL[slot][:, w], xh[:, x0 + k, :], xl[:, x0 + k, :],
                                first and k == 0, last and k == tiles - 1)
                return mm

            def project(n, j):
                if j == 1:
                    pe.wait_ge(misc_read, 4 * n - 1)
                else:
                    pe.wait_ge(proj_read, 3 * n + j)
                unit(j, n, MISC if j == 1 else PROJ, HH, HL).then_inc(unit_done[j], 1)

            def project_part(j, out_, k0, k1):
                mm = unit(j, 0, out_, HH, HL, x0=k0, tiles=k1 - k0, first=k0 == 0, last=k1 == KT, w0=k0)
                if k1 == KT:
                    mm.then_inc(unit_done[j], 1)

            def qk_sums(n, j, out_, hi_=SQH[:], lo_=SQL[:]):
                pe.wait_ge(qksl_done, 2 * n + (j + 1))
                nc.tensor.matmul(out_, PAIRONES[:], hi_, start=True, stop=False)
                nc.tensor.matmul(out_, PAIRONES[:], lo_, start=False, stop=True).then_inc(norm_done, 1)

            unit(0, 0, PROJ, HH, HL, step=0).then_inc(unit_done[0], 1)
            project_part(1, MISC, 0, 4)
            pe.wait_ge(ones_ready, 1)
            pe.wait_ge(xsum_done, KT - 1)
            nc.tensor.matmul(bank(0), ONES[:], SQSUM[:], start=True, stop=True).then_inc(stats_done, 1)
            project_part(1, MISC, 4, KT)
            pe.wait_ge(proj_read, 1)
            project_part(2, PROJ, 0, 3)
            pe.wait_ge(tri_ready, 3)
            qk_sums(0, 0, FIRST_SUMS[0])
            project_part(2, PROJ, 3, 5)
            qk_sums(0, 1, FIRST_SUMS[1], *FIRST_SQ[1][1:])
            project_part(2, PROJ, 5, KT)
            pe.wait_ge(const_ready, 6)
            pe.wait_ge(vzero, 2)

            def scores(a):
                pe.wait_ge(qkl_done, 2 * a + 2)
                for h in range(2):
                    hp = slice(h * HD, (h + 1) * HD)
                    for i in range(QB):
                        passes(Z[h][:, ZOFF[i]:ZOFF[i] + ZW[i]], QKH[1][hp, i * P:(i + 1) * P],
                               QKL[1][hp, i * P:(i + 1) * P], QKH[0][hp, i * P:], QKL[0][hp, i * P:],
                               start=i < 3, check=True)
                    for i in range(QB):
                        mm = nc.tensor.matmul(Z[h][:, ZOFF[i]:ZOFF[i] + P], IDENTB[:], MASKB[:], start=False,
                                              stop=True, skip_group_check=True)
                    mm.then_inc(z_done, 1)

            def turn_v(a):
                pe.wait_ge(proj_read, 3 * a + 3)
                pe.wait_ge(misc_read, 4 * a + 2)
                for b in range(QB):
                    mm = nc.tensor.transpose(MISC[:, b * P:(b + 1) * P], VT[:, b * P:(b + 1) * P], IDENT[:])
                mm.then_inc(vt_done, 1)

            def tails(a, h):
                pe.wait_ge(spl_done, 2 * a + (h + 1))
                for part in (AH[h], AL[h]):
                    for i in range(QB):
                        for j in range(i, QB):
                            mm = nc.tensor.matmul(Z[h][:, ZOFF[i] + (j - i) * P:ZOFF[i] + ZW[i]],
                                                  NEGTRI[:] if i == j else NEGONES[:],
                                                  part[:, ZOFF[j]:ZOFF[j] + ZW[j]],
                                                  start=False, stop=True, skip_group_check=True)
                mm.then_inc(tail_done, 1)

            def mix_values(a, read):
                pe.wait_ge(misc_read, read)
                for h in range(2):
                    pe.wait_ge(pl_done, 2 * a + (h + 1))
                    vh = VH[:, :, 2 * h:2 * h + 2, :].rearrange("p b h d -> p b (h d)")
                    vl = VL[:, :, 2 * h:2 * h + 2, :].rearrange("p b h d -> p b (h d)")
                    for i in range(QB):
                        z = slice(ZOFF[i], ZOFF[i] + ZW[i])
                        mm = passes(MISC[:, i * P:], vh[:, i, :], vl[:, i, :], AH[h][:, z], AL[h][:, z],
                                    start=h == 0 and i == 0, stop=h == 1 and i == QB - 1)
                mm.then_inc(o_done, 1)

            with pe.Fori(0, PAIRS - 1) as a:
                n = a + 1
                scores(a)
                turn_v(a)
                project(n, 0)
                project(n, 1)
                tails(a, 0)
                qk_sums(n, 0, PROJ)
                tails(a, 1)
                qk_sums(n, 1, MISC)
                project(n, 2)
                mix_values(a, 4 * a + 5)
            a = PAIRS - 1
            scores(a)
            turn_v(a)
            unit(0, USE_WO, RES[0], OH, OL, tiles=KT - 1, last=False)
            tails(a, 0)
            tails(a, 1)
            mix_values(a, 4 * a + 3)

            pe.wait_ge(misc_read, 4 * PAIRS)
            unit(0, USE_WO, RES[0], OH, OL, x0=KT - 1, tiles=1, first=False, w0=KT - 1).then_inc(unit_done[0], 1)
            unit(1, USE_WO, RES[1], OH, OL).then_inc(unit_done[1], 1)
            with pe.Fori(1, KT // 2) as i:
                for j in range(2):
                    pe.wait_ge(resid_done, 2 * i + (j - 1))
                    unit(j, i + USE_WO, RES[j], OH, OL).then_inc(unit_done[j], 1)

            def sum_squares():
                nc.tensor.matmul(MISC, ONES[:], SQSUM[:], start=True, stop=True).then_inc(stats_done, 1)

            def gate_up(layer, f):
                first = isinstance(f, int)
                if not (first and layer == 0):
                    pe.wait_ge(g_done, f + FT * layer)
                unit(0, f + USE_GU[layer], GATE, HH, HL, step=SPLIT_FFN[layer] if first else None)\
                    .then_inc(unit_done[0], 1)
                if first:
                    pe.wait_ge(sqsum_done, SUMS[2 * layer] + (KT - 1 if layer else KT + 1))
                    sum_squares()
                if not (first and layer == 0):
                    pe.wait_ge(u_done, f + FT * layer)
                unit(1, f + USE_GU[layer], UP, HH, HL).then_inc(unit_done[1], 1)

            def ffn(layer):
                gate_up(layer, 0)
                with pe.Fori(1, FT) as f:
                    gate_up(layer, f)

                def down(c, j, order=(0, 1, 2), uses=None):
                    pe.wait_ge(resid_done, c + (RES_DOWN[layer] - 1))
                    for u in order:
                        k0, k1 = DOWN_UNITS[u]
                        pe.wait_ge(fl_done, FT * layer + k1)
                        use = uses[u] if uses else c + (USE_DOWN2[layer] if u == 2 else USE_DOWN[layer])
                        unit(u, use, RES[j], FH, FL, x0=k0, tiles=k1 - k0, first=u == order[0], last=u == order[2])\
                            .then_inc(unit_done[u], 1)

                with pe.Fori(0, KT // 2 - (layer == 0)) as i:
                    for j in range(2):
                        down(2 * i + j, j)
                if layer == 0:
                    down(KT - 2, 0)
                    token_products(0)
                    token_products(1)
                    down(KT - 1, 1, (1, 2, 0), USE_LAST_DOWN)
                    token_products(2)

            def token_products(g):
                slot = g // 2
                if g == 3:
                    pe.wait_ge(ul_done, 1)
                pe.wait_ge(lo_ready[slot], USE_POOL[slot] + 1)
                for k in range(2):
                    pe.wait_ge(hl_done, SPLIT_POOL + 2 * g + k + 1)
                    w = slice((g % 2 * 2 + k) * GW, (g % 2 * 2 + k + 1) * GW)
                    for b in range(QB):
                        t = slice(b * P, (b + 1) * P)
                        mm = passes(TOK[g][:, b * GW:(b + 1) * GW], HH[:, 2 * g + k, t], HL[:, 2 * g + k, t],
                                    WH[slot][:, w], WL[slot][:, w], start=k == 0 and b % 2 == 0, stop=k == 1, check=True)
                mm.then_inc(unit_done[slot] if g % 2 else tok_done, 1)

            def token_stats():
                pe.wait_ge(sqsum_done, SUMS[1] + KT)
                pe.wait_ge(resid_done, 2 * KT)
                for b in range(QB):
                    nc.tensor.matmul(MISC[:, b:b + 1], SQSUM[:, b * P:(b + 1) * P], ONES[:, 0:1],
                                     start=b == 0, stop=False, skip_group_check=True)
                pe.wait_ge(last_sq, 1)
                for b in range(QB):
                    mm = nc.tensor.matmul(MISC[:, b:b + 1], A[:, b * P:(b + 1) * P], ONES[:, 0:1],
                                          start=False, stop=True, skip_group_check=True)
                mm.then_inc(stats_done, 1)

            def windows(c):
                g, ch = c // 2, c % 2 * P
                pe.wait_ge(ul_done, g + 1)
                pe.wait_ge(bandl_done, g + 1)
                if c >= KT - 2:
                    pe.wait_ge(resid_done, RES_POOL + c - 5)
                for b in range(QB):
                    cols = min(REACH, SEQ - b * P)
                    mm = passes(POOLED[c][:, b * P:b * P + cols], UH[:, g, b * GW + ch:b * GW + ch + P],
                                UL[:, g, b * GW + ch:b * GW + ch + P], BANDH[:, g, b, 0:cols], BANDL[:, g, b, 0:cols],
                                start=b == 0, stop=b == QB - 1, check=True)
                mm.then_inc(pool_done, 1)

            ffn(0)
            token_stats()
            token_products(3)
            for c in range(KT):
                windows(c)
            ffn(1)


def kernel(x, mix_norm, ffn_norm, attn_w_qkv, attn_q_norm, attn_k_norm, attn_w_o,
           pool_w, pool_scale, ffn_w_gu, ffn_w_down):
    import concourse.bacc as bacc
    from concourse.bass_utils import run_bass_kernel_spmd

    def tiles(v):
        return np.asarray(v).reshape(-1, P).T

    token, reached = np.arange(P)[:, None], np.arange(REACH)[None]
    table = np.array([[((reached >= token) & (reached < token + w)) / np.minimum(reached + 1 + P * later, w)
                       - (reached == token) for later in range(2)] for w in WINDOWS], np.float32)

    arrays = {
        "x": np.asarray(x).reshape(SEQ, KT, P).transpose(2, 1, 0),
        "vectors": np.concatenate([tiles(mix_norm), tiles(ffn_norm), tiles(pool_scale),
                                   tiles([np.asarray(attn_q_norm)] * 2), tiles([np.asarray(attn_k_norm)] * 2)], 1),
        "window_table": np.ascontiguousarray(table.transpose(2, 0, 1, 3)),
        "w_qkv": np.asarray(attn_w_qkv).reshape(KT, P, 3, PAIRS, P).transpose(3, 2, 1, 0, 4)
                   .reshape(PAIRS, 3, P, UK * P),
        "w_o": np.asarray(attn_w_o).reshape(KT, P, KT, P).transpose(2, 1, 0, 3).reshape(KT // 2, 2, P, UK * P),
        "w_gu": np.asarray(ffn_w_gu).reshape(2, KT, P, 2, FT, P).transpose(0, 4, 3, 2, 1, 5)
                  .reshape(2, FT, 2, P, UK * P),
        "w_down": np.asarray(ffn_w_down).reshape(2, FT, P, KT, P).transpose(0, 3, 2, 1, 4)
                    .reshape(2, KT, P, FT * P),
        "w_pool": np.asarray(pool_w).reshape(2, 2, 2, P, GW).transpose(0, 3, 1, 2, 4).reshape(2, P, UK * P),
    }
    nc = bacc.Bacc("TRN2", target_bir_lowering=False, num_devices=1)
    args, ins = [], {}
    for name, a in arrays.items():
        ins[f"in_{name}"] = np.ascontiguousarray(a)
        args.append(nc.dram_tensor(f"in_{name}", ins[f"in_{name}"].shape, F32, kind="ExternalInput").ap())
    out = nc.dram_tensor("out_y", (P, KT, SEQ), F32, kind="ExternalOutput").ap()
    build(nc, *args, out)
    r = run_bass_kernel_spmd(nc, [ins], core_ids=[0])
    y = np.asarray(r.results[0]["out_y"])
    return y.transpose(2, 1, 0).reshape(1, SEQ, D)
```

```python
from contextlib import ExitStack

import numpy as np

import concourse.bass as bass
from concourse import mybir

F32, F32R, BF16, I32 = mybir.dt.float32, mybir.dt.float32r, mybir.dt.bfloat16, mybir.dt.int32
ALU, ACT = mybir.AluOpType, mybir.ActivationFunctionType

P = 128
D, SEQ, HEADS, HD = 1024, 512, 16, 64
DFF = 2816
EPS = 1e-6
KT = D // P
FT = DFF // P
QB = SEQ // P
PAIRS = HEADS // 2
WINDOWS = (2, 4, 8, 16)
GW = D // len(WINDOWS)
REACH = P + max(WINDOWS)
UK = 8
DOWN_UNITS = ((0, 8), (8, 16), (16, FT))
MASKED = -1e30

ZOFF = (0, 512, 1024, 896)
ZW = tuple(SEQ - P * i for i in range(QB))
ZCOLS = sum(ZW)

USE_WO = PAIRS
USE_GU = (USE_WO + 3, USE_WO + 3 + FT + KT + 1)
USE_DOWN = (USE_GU[0] + FT, USE_GU[1] + FT)
USE_POOL = (USE_DOWN[0] + KT - 1, USE_DOWN[0] + KT)
USE_DOWN2 = (PAIRS + 2, PAIRS + 2 + KT)
USE_LAST_DOWN = (USE_DOWN[0] + KT, USE_DOWN[0] + KT - 1, USE_DOWN2[0] + KT - 1)
RES_WO, RES_DOWN, RES_POOL = 0, (KT, 3 * KT), 2 * KT
SPLIT_FFN, SPLIT_POOL = (KT, 3 * KT), 2 * KT
SUMS, SQUARES = (0, KT + 1, 2 * KT + 1), (0, KT)
V_MIX, V_FFN, V_SCALE, V_Q, V_K = 0, 2 * KT, 4 * KT, 5 * KT, 5 * KT + 1


def build(nc, x_in, vec_in, table_in, wqkv, wo, wgu, wdown, wpool, out):
    ctx = ExitStack()

    def sb(name, shape, dt=F32, where=ctx):
        return where.enter_context(nc.sbuf_tensor(name, shape, dt))

    def sem(name):
        return ctx.enter_context(nc.semaphore(name))

    with ctx:
        X = sb("X", [P, KT, SEQ])
        HH = sb("HH", [P, KT, SEQ], F32R)
        HL = sb("HL", [P, KT, SEQ], F32R)
        RAW = [sb(f"RAW{s}", [P, UK * P]) for s in range(3)]
        WH = [sb(f"WH{s}", [P, UK * P], F32R) for s in range(3)]
        WL = [sb(f"WL{s}", [P, UK * P], F32R) for s in range(3)]
        R = sb("R", [P, SEQ])
        SQ = sb("SQ", [P, SEQ])
        SQSUM = sb("SQSUM", [P, SEQ])
        VEC = sb("VEC", [P, 5 * KT + 2])
        RT = sb("RT", [P, QB, 1])
        EPSC = sb("EPSC", [P, 1])
        ONES = sb("ONES", [P, P])
        PAIRONESF = sb("PAIRONESF", [P, P])
        PAIRONES = sb("PAIRONES", [P, P], F32R)
        IDENT = sb("IDENT", [P, P])
        IDENTB = sb("IDENTB", [P, P], BF16)
        MASKB = sb("MASKB", [P, P], BF16)
        TRIF = sb("TRIF", [P, P])
        NEGTRI = sb("NEGTRI", [P, P], F32R)
        NEGBELOW = sb("NEGBELOW", [P, P], F32R)
        NEGONES = sb("NEGONES", [P, P], F32R)
        with ExitStack() as start:
            XSQ = sb("XSQ", [P, KT, SEQ], where=start)
        with ExitStack() as attn:
            OH = sb("OH", [P, PAIRS, SEQ], F32R, attn)
            OL = sb("OL", [P, PAIRS, SEQ], F32R, attn)
            QKF = [sb(f"{n}F", [P, SEQ], where=attn) for n in "QK"]
            QD = sb("QD", [P, 2, SEQ], F32R, attn)
            KS = sb("KS", [P, 2, SEQ], F32R, attn)
            QL = sb("QL", [P, SEQ], F32R, attn)
            VT = sb("VT", [P, SEQ], where=attn)
            VH = sb("VH", [P, QB, 4, HD], F32R, attn)
            VL = sb("VL", [P, QB, 4, HD], F32R, attn)
            RS = sb("RS", [P, SEQ], where=attn)
            SQH = sb("SQH", [P, SEQ], F32R, attn)
            SQL = sb("SQL", [P, SEQ], F32R, attn)
            E = [sb(f"E{h}", [P, ZCOLS], where=attn) for h in range(2)]
            SP = [sb(f"SP{h}", [P, ZCOLS], where=attn) for h in range(2)]
            AH = [sb(f"AH{h}", [P, ZCOLS], F32R, attn) for h in range(2)]
            AL = [sb(f"AL{h}", [P, ZCOLS], F32R, attn) for h in range(2)]
        FIRST_SQ = [(SQ[:], SQH[:], SQL[:]), (E[0][:, 0:SEQ], AH[0][:, 0:SEQ], AL[0][:, 0:SEQ])]
        FIRST_RS = [RS[:], E[1][:, 0:SEQ]]
        with ExitStack() as ffn:
            FH = sb("FH", [P, FT, SEQ], F32R, ffn)
            FL = sb("FL", [P, FT, SEQ], F32R, ffn)
            G = sb("G", [P, SEQ], where=ffn)
            S = sb("S", [P, SEQ], where=ffn)
            U = sb("U", [P, SEQ], where=ffn)
            A = sb("A", [P, SEQ], where=ffn)
        Y = [G, S]
        with ExitStack() as pool_mix:
            sb("FH_FIRST", [P, 2 * KT, SEQ], F32R, pool_mix)
            BAND = sb("BAND", [P, len(WINDOWS), QB, REACH], where=pool_mix)
            sb("FH_REST", [P, (FT - 2 * KT) * SEQ - len(WINDOWS) * QB * REACH], where=pool_mix)
            sb("FL_FIRST", [P, 2 * KT, SEQ], F32R, pool_mix)
            XSQ2 = sb("XSQ2", [P, QB, SEQ], where=pool_mix)
            sb("FL_REST", [P, FT - 2 * KT - QB, SEQ], where=pool_mix)
            TABLE = sb("TABLE", [P, len(WINDOWS), 2, REACH], where=pool_mix)
        UH = FH[:, KT:2 * KT, :].rearrange("p (g x) s -> p g (x s)", x=2)
        UL = FL[:, KT:2 * KT, :].rearrange("p (g x) s -> p g (x s)", x=2)

        def bands(tiles):
            flat = tiles.rearrange("p f s -> p (f s)")[:, 0:len(WINDOWS) * QB * REACH]
            return flat.rearrange("p (g b c) -> p g b c", g=len(WINDOWS), b=QB)

        BANDH, BANDL = bands(FH[:, 0:5, :]), bands(FL[:, 0:5, :])

        PS = ctx.enter_context(nc.psum_tensor("PS", [P, 8 * 512], F32))

        def bank(b, n=1):
            return PS[:, b * 512:(b + n) * 512]

        def ref_order(row):
            return row.rearrange("p (r b) -> p b r", b=QB)

        def own(h):
            return slice(h * HD, (h + 1) * HD)

        def by_block(row):
            return row.rearrange("p (b r) -> p b r", b=QB)

        Z = [bank(0, 3)[:, 0:ZCOLS], bank(3, 3)[:, 0:ZCOLS]]
        PROJ, MISC = bank(6), bank(7)
        RES = [bank(6), bank(7)]
        WO_OUT = [bank(6), bank(7), bank(1)]
        LAST_O = bank(0)
        TOK = [bank(0, 2), bank(2, 2), bank(4, 2), bank(0, 2)]
        POOLED = [bank(b) for b in (6, 7, 2, 3, 4, 5, 6, 7)]
        GATE, UP = bank(0), bank(1)
        FIRST_SUMS = (bank(1), bank(2))

        x_loaded = [sem(f"x_loaded{i}") for i in range(4)]
        vec_loaded, table_loaded = sem("vec_loaded"), sem("table_loaded")
        raw_full = [sem(f"raw_full{s}") for s in range(3)]
        hi_ready = [sem(f"hi_ready{s}") for s in range(3)]
        lo_ready = [sem(f"lo_ready{s}") for s in range(3)]
        unit_done = [sem(f"unit_done{s}") for s in range(3)]
        stored = [sem(f"stored{i}") for i in range(2)]
        made, const_ready, tri_ready, vzero = sem("made"), sem("const_ready"), sem("tri_ready"), sem("vzero")
        eps_ready, gain_ready, ones_ready = sem("eps_ready"), sem("gain_ready"), sem("ones_ready")
        xsq_done, xsq_even = sem("xsq_done"), sem("xsq_even")
        stats_done, ln_done, r_ready = sem("stats_done"), sem("ln_done"), sem("r_ready")
        hh_done, hl_done, xsum_done = sem("hh_done"), sem("hl_done"), sem("xsum_done")
        sq_one, sqsum_done = sem("sq_one"), sem("sqsum_done")
        resid_done = sem("resid_done")
        qksq_done, qksh_done = sem("qksq_done"), sem("qksh_done")
        qksl_done, norm_done = sem("qksl_done"), sem("norm_done")
        rs_done, qkn_done, qkh_done = sem("rs_done"), sem("qkn_done"), sem("qkh_done")
        qd_done, ql_done, kl_done = sem("qd_done"), sem("ql_done"), sem("kl_done")
        proj_read, misc_read = sem("proj_read"), sem("misc_read")
        vt_done, vh_done = sem("vt_done"), sem("vh_done")
        z_done, abs_done, exp_done, l_done = sem("z_done"), sem("abs_done"), sem("exp_done"), sem("l_done")
        sum2_done, sum1_done = sem("sum2_done"), sem("sum1_done")
        sp_done, sph_done, spl_done, tail_done = sem("sp_done"), sem("sph_done"), sem("spl_done"), sem("tail_done")
        prob_done, ph_done, pl_done = sem("prob_done"), sem("ph_done"), sem("pl_done")
        o_done, oh_done = sem("o_done"), sem("oh_done")
        g_done, s_done, u_done, a_done = sem("g_done"), sem("s_done"), sem("u_done"), sem("a_done")
        fh_done, fl_done = sem("fh_done"), sem("fl_done")
        tok_done, uh_done, ul_done, last_sq = sem("tok_done"), sem("uh_done"), sem("ul_done"), sem("last_sq")
        band_done, bandh_done, bandl_done = sem("band_done"), sem("bandh_done"), sem("bandl_done")
        bandl_late, pool_done = sem("bandl_late"), sem("pool_done")

        block = ctx.enter_context(nc.Block())

        @block.sync
        def _(sp):
            def load(slot, use, src, tiles=UK):
                if not (isinstance(use, int) and use == 0):
                    sp.wait_ge(lo_ready[slot], use)
                sp.dma_start(RAW[slot][:, 0:tiles * P], src).then_inc(raw_full[slot], 16)

            sp.dma_start(VEC[:], vec_in).then_inc(vec_loaded, 16)
            for i in range(4):
                sp.dma_start(X[:, 2 * i:2 * i + 2, :], x_in[:, 2 * i:2 * i + 2, :]).then_inc(x_loaded[i], 16)
                if i == 0:
                    load(0, 0, wqkv[0, 0])
            for j in range(1, 3):
                load(j, 0, wqkv[0, j])
            with sp.Fori(1, PAIRS) as n:
                for j in range(3):
                    load(j, n, wqkv[n, j])
            for c in range(KT):
                load(c % 3, USE_WO + c // 3, wo[c])
            for layer in range(2):
                with sp.Fori(0, FT) as f:
                    for j in range(2):
                        load(j, f + USE_GU[layer], wgu[layer, f, j])

                def down(c, order=(0, 1, 2)):
                    for j in order:
                        k0, k1 = DOWN_UNITS[j]
                        use = c + (USE_DOWN2[layer] if j == 2 else USE_DOWN[layer])
                        if layer == 0 and isinstance(c, int):
                            use = USE_LAST_DOWN[j]
                        load(j, use, wdown[layer, c, :, k0 * P:k1 * P], k1 - k0)

                with sp.Fori(0, KT - 1) as c:
                    down(c)
                if layer == 0:
                    load(0, USE_POOL[0], wpool[0])
                    sp.wait_ge(a_done, FT)
                    sp.dma_start(TABLE[:], table_in).then_inc(table_loaded, 16)
                    down(KT - 1, (1, 2, 0))
                    load(1, USE_POOL[1], wpool[1])
                else:
                    down(KT - 1)

        @block.gpsimd
        def _(pool):
            nc.gpsimd.memset(IDENT[:], 0.0).then_inc(made, 1)
            nc.gpsimd.memset(IDENTB[:], 0.0).then_inc(made, 1)
            nc.gpsimd.memset(MASKB[:], MASKED).then_inc(made, 1)
            nc.gpsimd.memset(TRIF[:], -1.0).then_inc(made, 1)
            nc.gpsimd.memset(PAIRONESF[:], 0.0).then_inc(made, 1)
            pool.wait_ge(made, 5)
            for t in (IDENT, IDENTB):
                nc.gpsimd.affine_select(out=t[:], in_=t[:], compare_op=ALU.not_equal, fill=1.0, base=0,
                                        pattern=[[-1, P]], channel_multiplier=1).then_inc(const_ready, 1)
            nc.gpsimd.affine_select(out=MASKB[:], in_=MASKB[:], compare_op=ALU.is_ge, fill=0.0, base=0,
                                    pattern=[[-1, P]], channel_multiplier=1).then_inc(const_ready, 1)
            nc.gpsimd.affine_select(out=TRIF[:], in_=TRIF[:], compare_op=ALU.is_ge, fill=0.0, base=0,
                                    pattern=[[-1, P]], channel_multiplier=1).then_inc(const_ready, 1)
            for h in range(2):
                pool.wait_ge(const_ready, 4 + h)
                nc.gpsimd.memset(PAIRONESF[h * HD:(h + 1) * HD, h * HD:(h + 1) * HD], 1.0).then_inc(const_ready, 1)
            for k in range(0, KT, 2):
                pool.wait_ge(const_ready, 6)
                pool.wait_ge(x_loaded[k // 2], 16)
                nc.gpsimd.tensor_tensor(XSQ[:, k, :], X[:, k, :], X[:, k, :], ALU.mult).then_inc(xsq_even, 1)
                if k:
                    pool.wait_ge(xsq_even, k)
                    nc.gpsimd.tensor_tensor(XSQ[:, 0, :], XSQ[:, 0, :], XSQ[:, k, :], ALU.add).then_inc(xsq_even, 1)
            nc.gpsimd.memset(VH[:].bitcast(F32), 0.0).then_inc(vzero, 1)
            nc.gpsimd.memset(VL[:].bitcast(F32), 0.0).then_inc(vzero, 1)

            def qk_square(n, j):
                if j == 0:
                    pool.wait_ge(proj_read, 3 * n + 1)
                else:
                    pool.wait_ge(misc_read, 4 * n)
                pool.wait_ge(qksl_done, 2 * n + j)
                nc.gpsimd.tensor_tensor(SQ[:], QKF[j][:], QKF[j][:], ALU.mult).then_inc(qksq_done, 1)
                pool.wait_ge(norm_done, 2 * n + j)
                pool.wait_ge(qksq_done, 2 * n + (j + 1))
                nc.gpsimd.tensor_tensor(SQH[:], QKF[j][:], QKF[j][:], ALU.mult).then_inc(qksh_done, 1)
                pool.wait_ge(qksh_done, 2 * n + (j + 1))
                nc.gpsimd.tensor_tensor(SQL[:], SQ[:], SQH[:].bitcast(F32), ALU.subtract).then_inc(qksl_done, 1)

            def q_lo(n):
                pool.wait_ge(qksl_done, 2 * n + 2)
                for h in range(2):
                    pool.wait_ge(qkh_done, 4 * n + (h + 1))
                    if h:
                        pool.wait_ge(ql_done, 2 * n + 1)
                    nc.gpsimd.tensor_tensor(QL[own(h), :], QKF[0][own(h), :], QD[own(h), h, :].bitcast(F32),
                                            ALU.subtract).then_inc(ql_done, 1)

            def lo(slot, use):
                pool.wait_ge(hi_ready[slot], use + 1)
                nc.gpsimd.tensor_tensor(WL[slot][:], RAW[slot][:], WH[slot][:].bitcast(F32), ALU.subtract)\
                    .then_inc(lo_ready[slot], 1)

            def weights_lo(use):
                pool.wait_ge(ql_done, 2 * use)
                lo(1, use)
                lo(2, use)

            lo(0, 1)
            with pool.Fori(1, PAIRS) as n:
                weights_lo(n)
                qk_square(n, 0)
                qk_square(n, 1)
                q_lo(n)
            weights_lo(USE_WO)

            def square_sum(round_, first, tiles):
                pool.wait_ge(stats_done, round_ + 1)
                if round_ == 0:
                    pool.wait_ge(qksl_done, 2 * PAIRS)
                nc.gpsimd.memset(SQSUM[:], 0.0).then_inc(sqsum_done, 1)
                with pool.Fori(0, tiles) as c:
                    pool.wait_ge(sqsum_done, c + (SUMS[round_] + 1))
                    pool.wait_ge(resid_done, c + (first + 1))
                    pool.wait_ge(vec_loaded, 16)
                    nc.gpsimd.tensor_tensor(SQ[:], X[:, c, :], X[:, c, :], ALU.mult).then_inc(sq_one, 1)
                    pool.wait_ge(sq_one, c + (SQUARES[round_] + 1))
                    nc.gpsimd.tensor_tensor(SQSUM[:], SQSUM[:], SQ[:], ALU.add).then_inc(sqsum_done, 1)

            def ffn_mul(layer):
                with pool.Fori(0, FT) as f:
                    pool.wait_ge(s_done, f + (FT * layer + 1))
                    pool.wait_ge(u_done, f + (FT * layer + 1))
                    nc.gpsimd.tensor_tensor(A[:], U[:], S[:], ALU.mult).then_inc(a_done, 1)

            square_sum(0, RES_WO, KT)
            ffn_mul(0)
            square_sum(1, RES_DOWN[0], KT - 1)
            pool.wait_ge(r_ready, 3)
            pool.wait_ge(unit_done[2], USE_LAST_DOWN[2] + 1)
            pool.wait_ge(table_loaded, 16)
            for g in range(len(WINDOWS)):
                nc.gpsimd.tensor_tensor(BAND[:, g, 0:1, :], TABLE[:, g, 0:1, :], RT[:, 0:1, :].to_broadcast([P, 1, REACH]),
                                        ALU.mult).then_inc(band_done, 1)
                nc.gpsimd.tensor_tensor(BAND[:, g, 1:QB, :], TABLE[:, g, 1:2, :].to_broadcast([P, QB - 1, REACH]),
                                        RT[:, 1:QB, :].to_broadcast([P, QB - 1, REACH]), ALU.mult)\
                    .then_inc(band_done, 1)
            for g in (2, 3):
                pool.wait_ge(bandh_done, g + 1)
                pool.wait_ge(band_done, 2 * len(WINDOWS))
                nc.gpsimd.tensor_tensor(BANDL[:, g], BAND[:, g], BANDH[:, g].bitcast(F32), ALU.subtract)\
                    .then_inc(bandl_late, 1)
            pool.wait_ge(stats_done, 3)
            for c in range(1, KT):
                pool.wait_ge(xsq_done, KT // 2 + c + 1)
                if c > 1:
                    pool.wait_ge(sqsum_done, SUMS[2] + c - 1)
                nc.gpsimd.tensor_tensor(SQSUM[:], XSQ2[:, 0, :] if c == 1 else SQSUM[:], XSQ2[:, c % QB, :], ALU.add)\
                    .then_inc(sqsum_done, 1)
            ffn_mul(1)

        @block.scalar
        def _(act):
            def hi(slot, use):
                act.wait_ge(raw_full[slot], 16 * use + 16)
                if not (isinstance(use, int) and use == 0):
                    act.wait_ge(unit_done[slot], use)
                nc.scalar.activation(WH[slot][:], RAW[slot][:], ACT.Copy).then_inc(hi_ready[slot], 1)

            def inverse_rms(src, n, round_, to=R[:]):
                act.wait_ge(stats_done, round_ + 1)
                nc.scalar.activation(to, src, ACT.Ln, bias=EPSC[:], scale=1.0 / n).then_inc(ln_done, 1)
                act.wait_ge(ln_done, round_ + 1)
                nc.scalar.activation(to, to, ACT.Exp, scale=-0.5).then_inc(r_ready, 1)

            nc.scalar.preload_act_table_set("natural_log_exp_and_others")
            act.wait_ge(eps_ready, 1)
            def start_square(k):
                nc.scalar.activation(XSQ[:, k, :], X[:, k, :], ACT.Square).then_inc(xsq_done, 1)

            act.wait_ge(vec_loaded, 16)
            for i in range(KT // 2):
                act.wait_ge(x_loaded[i], 16)
                for k in (2 * i, 2 * i + 1):
                    nc.scalar.activation(HH[:, k, :], X[:, k, :], ACT.Copy, scale=VEC[:, V_MIX + k:V_MIX + k + 1])\
                        .then_inc(hh_done, 1)
                if i == 0:
                    hi(0, 0)
                elif i < KT // 2 - 1:
                    start_square(2 * i - 1)
            hi(1, 0)
            start_square(KT - 3)
            start_square(KT - 1)
            act.wait_ge(const_ready, 6)
            nc.scalar.activation(NEGTRI[:], TRIF[:], ACT.Copy).then_inc(tri_ready, 1)
            nc.scalar.activation(PAIRONES[:], PAIRONESF[:], ACT.Copy).then_inc(tri_ready, 1)
            hi(2, 0)
            inverse_rms(bank(0), D, 0)

            def qk_rms(n, j, sums=(PROJ, MISC), rs=RS[:]):
                act.wait_ge(norm_done, 2 * n + (j + 1))
                if not isinstance(n, int):
                    act.wait_ge(qkn_done, 2 * n + j)
                if j == 0:
                    nc.scalar.activation(rs, sums[0], ACT.Ln, bias=EPSC[:], scale=1.0 / HD).then_inc(proj_read, 1)
                    act.wait_ge(proj_read, 3 * n + 2)
                else:
                    nc.scalar.activation(rs, sums[1], ACT.Ln, bias=EPSC[:], scale=1.0 / HD).then_inc(misc_read, 1)
                    act.wait_ge(misc_read, 2 if isinstance(n, int) else 4 * n + 1)
                nc.scalar.activation(rs, rs, ACT.Exp, scale=-0.5).then_inc(rs_done, 1)

            def qk_hi(n, j):
                for h in range(2):
                    act.wait_ge(qkn_done, 2 * n + (j + 1))
                    act.wait_ge(vec_loaded, 16)
                    nc.scalar.activation((QD, KS)[j][own(h), h, :], QKF[j][own(h), :], ACT.Copy).then_inc(qkh_done, 1)

            def q_again(n):
                for h in range(2):
                    act.wait_ge(qkn_done, 2 * n + 1)
                    act.wait_ge(vec_loaded, 16)
                    nc.scalar.activation(QD[own(1 - h), h, :], QKF[0][own(h), :], ACT.Copy).then_inc(qd_done, 1)

            for j in range(2):
                act.wait_ge((proj_read, misc_read)[j], 1)
                nc.scalar.activation(FIRST_SQ[j][0], QKF[j][:], ACT.Square).then_inc(qksq_done, 1)
                nc.scalar.activation(FIRST_SQ[j][1], QKF[j][:], ACT.Square).then_inc(qksh_done, 1)
            for j in range(2):
                qk_rms(0, j, FIRST_SUMS, FIRST_RS[j])
            for j in range(2):
                qk_hi(0, j)
            hi(0, 1)

            def score_exp(a, h):
                act.wait_ge(abs_done, 2 * a + (h + 1))
                nc.scalar.activation(E[h][:], E[h][:], ACT.Exp, scale=-1.0).then_inc(exp_done, 1)

            def score_ln(a, h):
                act.wait_ge(exp_done, 2 * a + (h + 1))
                nc.scalar.activation(E[h][:], E[h][:], ACT.Ln, bias=1.0).then_inc(l_done, 1)

            def v_hi(a):
                act.wait_ge(vt_done, a + 1)
                nc.scalar.activation(VH[:, :, 0:4:3, :], MISC.rearrange("p (b h d) -> p b h d", b=QB, h=2),
                                     ACT.Copy).then_inc(vh_done, 1)

            def probs(a, h):
                act.wait_ge(tail_done, 2 * a + (h + 1))
                nc.scalar.activation(E[h][:], Z[h], ACT.Exp).then_inc(prob_done, 1)

            def o_hi(a, src=MISC):
                act.wait_ge(o_done, a + 1)
                act.wait_ge(vec_loaded, 16)
                nc.scalar.activation(ref_order(OH[:, a, :]), by_block(src), ACT.Copy).then_inc(oh_done, 1)

            with act.Fori(0, PAIRS - 1) as a:
                n = a + 1
                hi(1, n)
                hi(2, n)
                score_exp(a, 0)
                v_hi(a)
                score_ln(a, 0)
                score_exp(a, 1)
                score_ln(a, 1)
                hi(0, n + 1)
                probs(a, 0)
                qk_rms(n, 0)
                probs(a, 1)
                qk_hi(n, 0)
                q_again(n)
                qk_rms(n, 1)
                qk_hi(n, 1)
                o_hi(a)
            a = PAIRS - 1
            hi(1, USE_WO)
            hi(2, USE_WO)
            score_exp(a, 0)
            v_hi(a)
            score_ln(a, 0)
            score_exp(a, 1)
            score_ln(a, 1)
            probs(a, 0)
            probs(a, 1)
            o_hi(a, LAST_O)

            def next_hi(c, first, gains):
                act.wait_ge(resid_done, c + (first + 1))
                act.wait_ge(vec_loaded, 16)
                nc.scalar.activation(HH[:, c, :], X[:, c, :], ACT.Copy, scale=VEC[:, bass.ds(gains + c, 1)])\
                    .then_inc(hh_done, 1)

            for c in range(KT):
                if c + 3 < KT:
                    hi(c % 3, USE_WO + c // 3 + 1)
                elif c % 3 == 0:
                    hi(0, USE_GU[0])
                next_hi(c, RES_WO, V_FFN)

            def f_hi(layer, f):
                act.wait_ge(a_done, f + (FT * layer + 1))
                act.wait_ge(vec_loaded, 16)
                nc.scalar.activation(FH[:, f, :], A[:], ACT.Copy).then_inc(fh_done, 1)

            def gate_up(layer, f):
                hi(1, f + USE_GU[layer])
                if not (isinstance(f, int) and f == 0):
                    f_hi(layer, f - 1)
                if isinstance(f, int):
                    inverse_rms(MISC, D, layer * 2 + 1)
                act.wait_ge(g_done, f + (FT * layer + 1))
                nc.scalar.activation(S[:], G[:], ACT.Silu).then_inc(s_done, 1)
                hi(0, f + (USE_GU[layer] + 1))

            def ffn(layer):
                gate_up(layer, 0)
                with act.Fori(1, FT) as f:
                    gate_up(layer, f)
                f_hi(layer, FT - 1)

                def down(c, last=False):
                    hi(1, c + USE_DOWN[layer])
                    hi(2, c + USE_DOWN2[layer])
                    if not last:
                        hi(0, c + (USE_DOWN[layer] + 1))

                def store(c, j):
                    act.wait_ge(resid_done, c + (RES_DOWN[1] + 1))
                    act.dma_start(out[:, c, :], Y[j][:]).then_inc(stored[j], 16)

                if layer == 0:
                    with act.Fori(0, KT - 2) as c:
                        down(c)
                        next_hi(c, RES_DOWN[0], V_MIX + KT)
                else:
                    with act.Fori(0, KT // 2 - 1) as i:
                        for j in range(2):
                            down(2 * i + j)
                            store(2 * i + j, j)
                    for j in range(2):
                        down(KT - 2 + j, last=j == 1)
                        store(KT - 2 + j, j)
                    for j in range(2):
                        act.wait_ge(stored[j], 16 * (KT // 2))

            ffn(0)
            hi(1, USE_DOWN[0] + KT - 2)
            hi(2, USE_DOWN2[0] + KT - 2)
            hi(0, USE_POOL[0])
            next_hi(KT - 2, RES_DOWN[0], V_MIX + KT)
            hi(1, USE_LAST_DOWN[1])
            hi(2, USE_LAST_DOWN[2])
            hi(0, USE_LAST_DOWN[0])
            hi(1, USE_POOL[1])
            nc.scalar.preload_act_table_set("natural_log_exp_and_others")

            def token_hi(g):
                if g % 2:
                    act.wait_ge(unit_done[g // 2], USE_POOL[g // 2] + 1)
                else:
                    act.wait_ge(tok_done, g // 2 + 1)
                act.wait_ge(unit_done[1], USE_LAST_DOWN[1] + 1)
                nc.scalar.activation(UH[:, g, :], TOK[g], ACT.Copy).then_inc(uh_done, 1)

            def band_hi(g):
                act.wait_ge(band_done, 2 * g + 2)
                act.wait_ge(unit_done[0], USE_LAST_DOWN[0] + 1)
                nc.scalar.activation(BANDH[:, g], BAND[:, g], ACT.Copy).then_inc(bandh_done, 1)

            def pool_square(c):
                if c >= QB:
                    act.wait_ge(sqsum_done, SUMS[2] + c - QB + (c == QB))
                nc.scalar.activation(XSQ2[:, c % QB, :], X[:, c, :], ACT.Square).then_inc(xsq_done, 1)

            token_hi(0)
            token_hi(1)
            act.wait_ge(resid_done, 2 * KT)
            nc.scalar.activation(A[:], X[:, KT - 1, :], ACT.Square).then_inc(last_sq, 1)
            next_hi(KT - 1, RES_DOWN[0], V_MIX + KT)
            hi(0, USE_GU[1])
            inverse_rms(bank(6)[:, 0:QB], D, 2, RT[:, :, 0])
            band_hi(0)
            token_hi(2)
            band_hi(1)
            band_hi(2)
            token_hi(3)
            band_hi(3)
            next_hi(0, RES_POOL, V_FFN + KT)
            pool_square(0)
            for c in range(1, KT):
                next_hi(c, RES_POOL, V_FFN + KT)
                pool_square(c)
            ffn(1)

        @block.vector
        def _(dve):
            def lo(slot, use):
                dve.wait_ge(hi_ready[slot], use + 1)
                nc.vector.tensor_tensor(WL[slot][:], RAW[slot][:], WH[slot][:].bitcast(F32), ALU.subtract)\
                    .then_inc(lo_ready[slot], 1)

            nc.vector.memset(EPSC[:], EPS).then_inc(eps_ready, 1)
            nc.vector.memset(ONES[:], 1.0).then_inc(ones_ready, 1)
            nc.vector.memset(NEGONES[:].bitcast(F32), -1.0).then_inc(tri_ready, 1)
            dve.wait_ge(vec_loaded, 16)

            def add_square(k):
                if k == KT:
                    dve.wait_ge(xsq_even, KT - 1)
                else:
                    dve.wait_ge(xsq_done, (k + 1) // 2)
                if k > 3:
                    dve.wait_ge(xsum_done, k // 2 - 1)
                nc.vector.tensor_tensor(SQSUM[:], XSQ[:, 1, :] if k == 3 else SQSUM[:], XSQ[:, k % KT, :], ALU.add)\
                    .then_inc(xsum_done, 1)

            nc.vector.tensor_scalar(VEC[:, V_Q:V_Q + 1], VEC[:, V_Q:V_Q + 1], HD ** -0.5, None, ALU.mult)\
                .then_inc(gain_ready, 1)
            for k in range(KT):
                dve.wait_ge(hh_done, k + 1)
                nc.vector.scalar_tensor_tensor(HL[:, k, :], X[:, k, :], VEC[:, V_MIX + k:V_MIX + k + 1],
                                               HH[:, k, :].bitcast(F32), ALU.mult, ALU.subtract).then_inc(hl_done, 1)
                if k == 1:
                    lo(0, 0)
                if k == 5:
                    add_square(3)
            lo(1, 0)
            dve.wait_ge(const_ready, 6)
            nc.vector.tensor_scalar(NEGBELOW[:], TRIF[:], -1.0, -1.0, ALU.mult, ALU.add).then_inc(tri_ready, 1)
            add_square(5)
            add_square(7)
            add_square(KT)
            lo(2, 0)

            def scale_qk(n, j):
                dve.wait_ge(unit_done[j], n + 1)
                if isinstance(n, int):
                    dve.wait_ge(r_ready, 1)
                elif j == 0:
                    dve.wait_ge(ql_done, 2 * n)
                nc.vector.tensor_tensor(QKF[j][:], (PROJ, MISC)[j], R[:], ALU.mult)\
                    .then_inc((proj_read, misc_read)[j], 1)

            def scale_v(n):
                dve.wait_ge(unit_done[2], n + 1)
                nc.vector.tensor_tensor(VT[:], PROJ, R[:], ALU.mult).then_inc(proj_read, 1)

            def qk_norm(n, j, rs=RS[:]):
                dve.wait_ge(rs_done, 2 * n + (j + 1))
                dve.wait_ge(gain_ready, 1)
                nc.vector.scalar_tensor_tensor(QKF[j][:], QKF[j][:], VEC[:, V_Q + j:V_Q + j + 1], rs,
                                               ALU.mult, ALU.mult).then_inc(qkn_done, 1)

            def first_lo(j):
                whole, hi_, lo_ = FIRST_SQ[j]
                dve.wait_ge(qksh_done, j + 1)
                nc.vector.tensor_tensor(lo_, whole, hi_.bitcast(F32), ALU.subtract).then_inc(qksl_done, 1)

            def first_q_again():
                for h in range(2):
                    dve.wait_ge(qkn_done, 1)
                    nc.vector.tensor_copy(QD[own(1 - h), h, :], QKF[0][own(h), :]).then_inc(qd_done, 1)

            def first_q_lo(h):
                dve.wait_ge(qkh_done, h + 1)
                nc.vector.tensor_tensor(QL[own(h), :], QKF[0][own(h), :], QD[own(h), h, :].bitcast(F32),
                                        ALU.subtract).then_inc(ql_done, 1)

            def k_lo(n, h):
                dve.wait_ge(qkh_done, 4 * n + (h + 3))
                nc.vector.tensor_tensor(KS[own(1 - h), h, :], QKF[1][own(h), :], KS[own(h), h, :].bitcast(F32),
                                        ALU.subtract).then_inc(kl_done, 1)

            scale_qk(0, 0)
            first_lo(0)
            scale_qk(0, 1)
            first_lo(1)
            qk_norm(0, 0, FIRST_RS[0])
            first_q_again()
            qk_norm(0, 1, FIRST_RS[1])
            for h in range(2):
                first_q_lo(h)
                k_lo(0, h)
            scale_v(0)

            def score_abs(a, h):
                dve.wait_ge(z_done, 2 * a + (h + 1))
                nc.vector.tensor_scalar(E[h][:].bitcast(I32), Z[h].bitcast(I32), 0x7FFFFFFF, None, ALU.bitwise_and)\
                    .then_inc(abs_done, 1)

            def softplus(a, h):
                dve.wait_ge(l_done, 2 * a + (h + 1))
                nc.vector.scalar_tensor_tensor(SP[h][:], Z[h], 0.0, E[h][:], ALU.max, ALU.add).then_inc(sp_done, 1)
                for i, done in ((2, sp_done), (1, sum2_done)):
                    own = SP[h][:, ZOFF[i] + P:ZOFF[i] + ZW[i]]
                    dve.wait_ge(done, 2 * a + (h + 1))
                    nc.vector.tensor_tensor(own, own, SP[h][:, ZOFF[i + 1]:ZOFF[i + 1] + ZW[i + 1]], ALU.add)\
                        .then_inc(sum2_done if i == 2 else sum1_done, 1)
                dve.wait_ge(sum1_done, 2 * a + (h + 1))
                nc.vector.tensor_copy(AH[h][:], SP[h][:]).then_inc(sph_done, 1)
                dve.wait_ge(sph_done, 2 * a + (h + 1))
                nc.vector.tensor_tensor(AL[h][:], SP[h][:], AH[h][:].bitcast(F32), ALU.subtract).then_inc(spl_done, 1)

            def v_lo(a):
                dve.wait_ge(vh_done, a + 1)
                nc.vector.tensor_tensor(VL[:, :, 0:4:3, :], MISC.rearrange("p (b h d) -> p b h d", b=QB, h=2),
                                        VH[:, :, 0:4:3, :].bitcast(F32), ALU.subtract).then_inc(misc_read, 1)

            def probs_split(a, h):
                dve.wait_ge(prob_done, 2 * a + (h + 1))
                nc.vector.tensor_copy(AH[h][:], E[h][:]).then_inc(ph_done, 1)
                dve.wait_ge(ph_done, 2 * a + (h + 1))
                nc.vector.tensor_tensor(AL[h][:], E[h][:], AH[h][:].bitcast(F32), ALU.subtract).then_inc(pl_done, 1)

            def o_lo(a, src=MISC):
                dve.wait_ge(oh_done, a + 1)
                nc.vector.tensor_tensor(ref_order(OL[:, a, :]), by_block(src), ref_order(OH[:, a, :].bitcast(F32)),
                                        ALU.subtract)\
                    .then_inc(misc_read, 1)

            with dve.Fori(0, PAIRS - 1) as a:
                n = a + 1
                score_abs(a, 0)
                score_abs(a, 1)
                v_lo(a)
                softplus(a, 0)
                scale_qk(n, 0)
                softplus(a, 1)
                scale_qk(n, 1)
                lo(0, n + 1)
                probs_split(a, 0)
                qk_norm(n, 0)
                probs_split(a, 1)
                qk_norm(n, 1)
                scale_v(n)
                k_lo(n, 0)
                k_lo(n, 1)
                o_lo(a)
            a = PAIRS - 1
            score_abs(a, 0)
            score_abs(a, 1)
            v_lo(a)
            softplus(a, 0)
            softplus(a, 1)
            probs_split(a, 0)
            probs_split(a, 1)
            o_lo(a, LAST_O)

            def residual(c, done_sem, done, src):
                dve.wait_ge(done_sem, done)
                nc.vector.tensor_tensor(X[:, c, :], src, X[:, c, :], ALU.add).then_inc(resid_done, 1)

            def next_lo(c, before, gains):
                dve.wait_ge(hh_done, c + (before + 1))
                nc.vector.scalar_tensor_tensor(HL[:, c, :], X[:, c, :], VEC[:, bass.ds(gains + c, 1)],
                                               HH[:, c, :].bitcast(F32), ALU.mult, ALU.subtract).then_inc(hl_done, 1)

            for c in range(KT):
                residual(c, unit_done[c % 3], USE_WO + c // 3 + 1, WO_OUT[c % 3])
                if c + 3 < KT:
                    lo(c % 3, USE_WO + c // 3 + 1)
                elif c % 3 == 0:
                    lo(0, USE_GU[0])
                next_lo(c, SPLIT_FFN[0], V_FFN)

            def f_lo(layer, f):
                dve.wait_ge(fh_done, f + (FT * layer + 1))
                nc.vector.tensor_tensor(FL[:, f, :], A[:], FH[:, f, :].bitcast(F32), ALU.subtract).then_inc(fl_done, 1)

            def gate_up(layer, f):
                lo(1, f + USE_GU[layer])
                if not (isinstance(f, int) and f == 0):
                    f_lo(layer, f - 1)
                if isinstance(f, int):
                    dve.wait_ge(r_ready, layer * 2 + 2)
                dve.wait_ge(unit_done[0], f + (USE_GU[layer] + 1))
                nc.vector.tensor_tensor(G[:], GATE, R[:], ALU.mult).then_inc(g_done, 1)
                lo(0, f + (USE_GU[layer] + 1))
                dve.wait_ge(unit_done[1], f + (USE_GU[layer] + 1))
                nc.vector.tensor_tensor(U[:], UP, R[:], ALU.mult).then_inc(u_done, 1)

            def ffn(layer):
                gate_up(layer, 0)
                with dve.Fori(1, FT) as f:
                    gate_up(layer, f)
                f_lo(layer, FT - 1)

                def down(c, j, last=False):
                    lo(1, c + USE_DOWN[layer])
                    lo(2, c + USE_DOWN2[layer])
                    if not last:
                        lo(0, c + (USE_DOWN[layer] + 1))
                    done = c + (USE_DOWN2[layer] + 1)
                    if layer == 0:
                        residual(c, unit_done[2], done, RES[j])
                        next_lo(c, SPLIT_POOL, V_MIX + KT)
                    else:
                        if not (isinstance(c, int) and c == j):
                            dve.wait_ge(stored[j], (c - j) * 8)
                        dve.wait_ge(unit_done[2], done)
                        nc.vector.tensor_tensor(Y[j][:], RES[j], X[:, c, :], ALU.add).then_inc(resid_done, 1)

                if layer == 0:
                    with dve.Fori(0, KT // 2 - 1) as i:
                        for j in range(2):
                            down(2 * i + j, j)
                else:
                    for j in range(2):
                        down(j, j)
                    with dve.Fori(1, KT // 2 - 1) as i:
                        for j in range(2):
                            down(2 * i + j, j)
                    for j in range(2):
                        down(KT - 2 + j, j, last=j == 1)

            ffn(0)
            lo(1, USE_DOWN[0] + KT - 2)
            lo(2, USE_DOWN2[0] + KT - 2)
            lo(0, USE_POOL[0])
            residual(KT - 2, unit_done[2], USE_DOWN2[0] + KT - 1, RES[0])
            next_lo(KT - 2, SPLIT_POOL, V_MIX + KT)
            lo(1, USE_LAST_DOWN[1])
            lo(2, USE_LAST_DOWN[2])
            lo(0, USE_LAST_DOWN[0])
            lo(1, USE_POOL[1])

            def token_lo(g):
                dve.wait_ge(uh_done, g + 1)
                nc.vector.tensor_tensor(UL[:, g, :], TOK[g], UH[:, g, :].bitcast(F32), ALU.subtract)\
                    .then_inc(ul_done, 1)

            def band_lo(g):
                dve.wait_ge(bandh_done, g + 1)
                nc.vector.tensor_tensor(BANDL[:, g], BAND[:, g], BANDH[:, g].bitcast(F32), ALU.subtract)\
                    .then_inc(bandl_done, 1)

            def pool_residual(c):
                dve.wait_ge(pool_done, c + 1)
                nc.vector.scalar_tensor_tensor(X[:, c, :], POOLED[c], VEC[:, V_SCALE + c:V_SCALE + c + 1], X[:, c, :],
                                               ALU.mult, ALU.add).then_inc(resid_done, 1)

            token_lo(0)
            token_lo(1)
            residual(KT - 1, unit_done[0], USE_LAST_DOWN[0] + 1, RES[1])
            next_lo(KT - 1, SPLIT_POOL, V_MIX + KT)
            lo(0, USE_GU[1])
            band_lo(0)
            token_lo(2)
            band_lo(1)
            pool_residual(0)
            token_lo(3)
            pool_residual(1)
            next_lo(0, SPLIT_FFN[1], V_FFN + KT)
            for c in range(2, KT):
                pool_residual(c)
                next_lo(c - 1, SPLIT_FFN[1], V_FFN + KT)
            next_lo(KT - 1, SPLIT_FFN[1], V_FFN + KT)
            ffn(1)

        @block.tensor
        def _(pe):
            def passes(out_, wh, wl, xh, xl, start, stop=False, check=False):
                nc.tensor.matmul(out_, wh, xh, start=start, stop=False, skip_group_check=check)
                nc.tensor.matmul(out_, wh, xl, start=False, stop=False, skip_group_check=check)
                return nc.tensor.matmul(out_, wl, xh, start=False, stop=stop, skip_group_check=check)

            def unit(slot, use, out_, xh, xl, x0=0, tiles=UK, first=True, last=True, step=None, w0=0):
                pe.wait_ge(lo_ready[slot], use + 1)
                for k in range(tiles):
                    if step is not None:
                        pe.wait_ge(hl_done, step + k + 1)
                    w = slice((w0 + k) * P, (w0 + k + 1) * P)
                    mm = passes(out_, WH[slot][:, w], WL[slot][:, w], xh[:, x0 + k, :], xl[:, x0 + k, :],
                                first and k == 0, last and k == tiles - 1)
                return mm

            def project(n, j):
                if j == 1:
                    pe.wait_ge(misc_read, 4 * n - 1)
                else:
                    pe.wait_ge(proj_read, 3 * n)
                unit(j, n, MISC if j == 1 else PROJ, HH, HL).then_inc(unit_done[j], 1)

            def project_part(j, out_, k0, k1):
                mm = unit(j, 0, out_, HH, HL, x0=k0, tiles=k1 - k0, first=k0 == 0, last=k1 == KT, w0=k0)
                if k1 == KT:
                    mm.then_inc(unit_done[j], 1)

            def qk_sums(n, j, out_, hi_=SQH[:], lo_=SQL[:]):
                pe.wait_ge(qksl_done, 2 * n + (j + 1))
                nc.tensor.matmul(out_, PAIRONES[:], hi_, start=True, stop=False)
                nc.tensor.matmul(out_, PAIRONES[:], lo_, start=False, stop=True).then_inc(norm_done, 1)

            def keep_warm(times):
                for _ in range(times):
                    nc.tensor.matmul(bank(5)[:, 0:P], ONES[:], ONES[:], start=True, stop=True)

            pe.wait_ge(ones_ready, 1)
            keep_warm(24)
            unit(0, 0, PROJ, HH, HL, step=0).then_inc(unit_done[0], 1)
            project_part(1, MISC, 0, 3)
            pe.wait_ge(xsum_done, KT // 2)
            nc.tensor.matmul(bank(0), ONES[:], SQSUM[:], start=True, stop=True).then_inc(stats_done, 1)
            project_part(1, MISC, 3, KT)
            pe.wait_ge(proj_read, 1)
            project_part(2, PROJ, 0, 3)
            pe.wait_ge(tri_ready, 4)
            qk_sums(0, 0, FIRST_SUMS[0])
            project_part(2, PROJ, 3, 5)
            qk_sums(0, 1, FIRST_SUMS[1], *FIRST_SQ[1][1:])
            project_part(2, PROJ, 5, KT)
            keep_warm(6)
            pe.wait_ge(const_ready, 6)
            pe.wait_ge(vzero, 2)

            def scores(a):
                for h in range(2):
                    pe.wait_ge(ql_done, 2 * a + (h + 1))
                    pe.wait_ge(qd_done, 2 * a + (h + 1))
                    pe.wait_ge(kl_done, 2 * a + (h + 1))
                    for i in range(QB):
                        z, keys = Z[h][:, ZOFF[i]:ZOFF[i] + ZW[i]], slice(i * P, (i + 1) * P)
                        nc.tensor.matmul(z, KS[:, h, keys], QD[:, h, i * P:], start=i < 3, stop=False,
                                         skip_group_check=True)
                        nc.tensor.matmul(z, KS[own(h), h, keys], QL[own(h), i * P:], start=False, stop=False,
                                         skip_group_check=True)
                    for i in range(QB):
                        mm = nc.tensor.matmul(Z[h][:, ZOFF[i]:ZOFF[i] + P], IDENTB[:], MASKB[:], start=False,
                                              stop=True, skip_group_check=True)
                    mm.then_inc(z_done, 1)

            def turn_v(a):
                pe.wait_ge(proj_read, 3 * a + 3)
                pe.wait_ge(misc_read, 4 * a + 2)
                for b in range(QB):
                    mm = nc.tensor.transpose(MISC[:, b * P:(b + 1) * P], VT[:, b * P:(b + 1) * P], IDENT[:])
                mm.then_inc(vt_done, 1)

            def tails(a, h):
                pe.wait_ge(spl_done, 2 * a + (h + 1))
                for part in (AH[h], AL[h]):
                    for i in range(QB):
                        for j in range(i, min(i + 2, QB)):
                            later = NEGBELOW if i else NEGONES
                            mm = nc.tensor.matmul(Z[h][:, ZOFF[i] + (j - i) * P:ZOFF[i] + ZW[i]],
                                                  NEGTRI[:] if i == j else later[:],
                                                  part[:, ZOFF[j]:ZOFF[j] + ZW[j]],
                                                  start=False, stop=True, skip_group_check=True)
                mm.then_inc(tail_done, 1)

            def mix_values(a, out_=MISC, heads=range(2)):
                for h in heads:
                    pe.wait_ge(pl_done, 2 * a + (h + 1))
                    vh = VH[:, :, 2 * h:2 * h + 2, :].rearrange("p b h d -> p b (h d)")
                    vl = VL[:, :, 2 * h:2 * h + 2, :].rearrange("p b h d -> p b (h d)")
                    for i in range(QB):
                        z = slice(ZOFF[i], ZOFF[i] + ZW[i])
                        mm = passes(out_[:, i * P:], vh[:, i, :], vl[:, i, :], AH[h][:, z], AL[h][:, z],
                                    start=h == 0 and i == 0, stop=h == 1 and i == QB - 1)
                if h == 1:
                    mm.then_inc(o_done, 1)

            with pe.Fori(0, PAIRS - 1) as a:
                n = a + 1
                scores(a)
                turn_v(a)
                project(n, 0)
                project(n, 1)
                tails(a, 0)
                qk_sums(n, 0, PROJ)
                tails(a, 1)
                pe.wait_ge(proj_read, 3 * n + 2)
                unit(2, n, PROJ, HH, HL, tiles=4, last=False)
                qk_sums(n, 1, MISC)
                unit(2, n, PROJ, HH, HL, x0=4, tiles=KT - 4, first=False, w0=4).then_inc(unit_done[2], 1)
                pe.wait_ge(misc_read, 4 * a + 5)
                mix_values(a)
            a = PAIRS - 1
            scores(a)
            turn_v(a)
            def output_part(c, k0, k1):
                mm = unit(c % 3, USE_WO + c // 3, WO_OUT[c % 3], OH, OL, x0=k0, tiles=k1 - k0, first=k0 == 0,
                          last=k1 == KT, w0=k0)
                if k1 == KT:
                    mm.then_inc(unit_done[c % 3], 1)

            output_part(0, 0, KT - 1)
            pe.wait_ge(misc_read, 4 * a + 3)
            output_part(1, 0, 5)
            tails(a, 0)
            output_part(1, 5, KT - 1)
            tails(a, 1)
            pe.wait_ge(prob_done, 2 * a + 1)
            output_part(2, 0, 3)
            mix_values(a, LAST_O, (0,))
            output_part(2, 3, 4)
            mix_values(a, LAST_O, (1,))
            output_part(2, 4, 6)

            pe.wait_ge(misc_read, 4 * PAIRS)
            output_part(0, KT - 1, KT)
            output_part(1, KT - 1, KT)
            output_part(2, 6, KT)
            for c in range(3, KT):
                pe.wait_ge(resid_done, c - 2)
                output_part(c, 0, KT)

            def sum_squares():
                nc.tensor.matmul(MISC, ONES[:], SQSUM[:], start=True, stop=True).then_inc(stats_done, 1)

            def gate_up(layer, f):
                first = isinstance(f, int)
                if not (first and layer == 0):
                    pe.wait_ge(g_done, f + FT * layer)
                unit(0, f + USE_GU[layer], GATE, HH, HL, step=SPLIT_FFN[layer] if first else None)\
                    .then_inc(unit_done[0], 1)
                if first:
                    pe.wait_ge(sqsum_done, SUMS[2 * layer] + (KT - 1 if layer else KT + 1))
                    sum_squares()
                if not (first and layer == 0):
                    pe.wait_ge(u_done, f + FT * layer)
                unit(1, f + USE_GU[layer], UP, HH, HL).then_inc(unit_done[1], 1)

            def ffn(layer):
                gate_up(layer, 0)
                with pe.Fori(1, FT) as f:
                    gate_up(layer, f)

                def down(c, j, order=(0, 1, 2), uses=None):
                    pe.wait_ge(resid_done, c + (RES_DOWN[layer] - 1))
                    for u in order:
                        k0, k1 = DOWN_UNITS[u]
                        pe.wait_ge(fl_done, FT * layer + k1)
                        use = uses[u] if uses else c + (USE_DOWN2[layer] if u == 2 else USE_DOWN[layer])
                        unit(u, use, RES[j], FH, FL, x0=k0, tiles=k1 - k0, first=u == order[0], last=u == order[2])\
                            .then_inc(unit_done[u], 1)

                with pe.Fori(0, KT // 2 - (layer == 0)) as i:
                    for j in range(2):
                        down(2 * i + j, j)
                if layer == 0:
                    down(KT - 2, 0)
                    token_products(0)
                    token_products(1)
                    down(KT - 1, 1, (1, 2, 0), USE_LAST_DOWN)

            def token_products(g, rows=(0, 1)):
                slot = g // 2
                if g == 3:
                    pe.wait_ge(ul_done, 1)
                pe.wait_ge(lo_ready[slot], USE_POOL[slot] + 1)
                for k in rows:
                    pe.wait_ge(hl_done, SPLIT_POOL + 2 * g + k + 1)
                    w = slice((g % 2 * 2 + k) * GW, (g % 2 * 2 + k + 1) * GW)
                    for b in range(QB):
                        t = slice(b * P, (b + 1) * P)
                        mm = passes(TOK[g][:, b * GW:(b + 1) * GW], HH[:, 2 * g + k, t], HL[:, 2 * g + k, t],
                                    WH[slot][:, w], WL[slot][:, w], start=k == 0 and b % 2 == 0, stop=k == 1, check=True)
                if rows[-1] == 1:
                    mm.then_inc(unit_done[slot] if g % 2 else tok_done, 1)

            def token_stats(squares, first, last):
                for b in range(QB):
                    mm = nc.tensor.matmul(bank(6)[:, b:b + 1], squares[:, b * P:(b + 1) * P], ONES[:, 0:1],
                                          start=first and b == 0, stop=last, skip_group_check=True)
                return mm

            def windows(c):
                g, ch = c // 2, c % 2 * P
                pe.wait_ge(ul_done, g + 1)
                if g < 2:
                    pe.wait_ge(bandl_done, g + 1)
                else:
                    pe.wait_ge(bandl_late, g - 1)
                if c >= KT - 2:
                    pe.wait_ge(resid_done, RES_POOL + c - 5)
                for b in range(QB):
                    cols = min(REACH, SEQ - b * P)
                    mm = passes(POOLED[c][:, b * P:b * P + cols], UH[:, g, b * GW + ch:b * GW + ch + P],
                                UL[:, g, b * GW + ch:b * GW + ch + P], BANDH[:, g, b, 0:cols], BANDL[:, g, b, 0:cols],
                                start=b == 0, stop=b == QB - 1, check=True)
                mm.then_inc(pool_done, 1)

            ffn(0)
            pe.wait_ge(sqsum_done, SUMS[1] + KT)
            pe.wait_ge(resid_done, 2 * KT - 1)
            token_stats(SQSUM, True, False)
            token_products(2, (0,))
            pe.wait_ge(last_sq, 1)
            token_stats(A, False, True).then_inc(stats_done, 1)
            token_products(2, (1,))
            token_products(3)
            for c in range(KT):
                windows(c)
            ffn(1)


def kernel(x, mix_norm, ffn_norm, attn_w_qkv, attn_q_norm, attn_k_norm, attn_w_o,
           pool_w, pool_scale, ffn_w_gu, ffn_w_down):
    import concourse.bacc as bacc
    from concourse.bass_utils import run_bass_kernel_spmd

    def tiles(v):
        return np.asarray(v).reshape(-1, P).T

    token, reached = np.arange(P)[:, None], np.arange(REACH)[None]
    table = np.array([[((reached >= token) & (reached < token + w)) / np.minimum(reached + 1 + P * later, w)
                       - (reached == token) for later in range(2)] for w in WINDOWS], np.float32)

    arrays = {
        "x": np.asarray(x).reshape(SEQ, KT, P).transpose(2, 1, 0),
        "vectors": np.concatenate([tiles(mix_norm), tiles(ffn_norm), tiles(pool_scale),
                                   tiles([np.asarray(attn_q_norm)] * 2), tiles([np.asarray(attn_k_norm)] * 2)], 1),
        "window_table": np.ascontiguousarray(table.transpose(2, 0, 1, 3)),
        "w_qkv": np.asarray(attn_w_qkv).reshape(KT, P, 3, PAIRS, P).transpose(3, 2, 1, 0, 4)
                   .reshape(PAIRS, 3, P, UK * P),
        "w_o": np.asarray(attn_w_o).reshape(KT, P, KT, P).transpose(2, 1, 0, 3).reshape(KT, P, UK * P),
        "w_gu": np.asarray(ffn_w_gu).reshape(2, KT, P, 2, FT, P).transpose(0, 4, 3, 2, 1, 5)
                  .reshape(2, FT, 2, P, UK * P),
        "w_down": np.asarray(ffn_w_down).reshape(2, FT, P, KT, P).transpose(0, 3, 2, 1, 4)
                    .reshape(2, KT, P, FT * P),
        "w_pool": np.asarray(pool_w).reshape(2, 2, 2, P, GW).transpose(0, 3, 1, 2, 4).reshape(2, P, UK * P),
    }
    nc = bacc.Bacc("TRN2", target_bir_lowering=False, num_devices=1)
    args, ins = [], {}
    for name, a in arrays.items():
        ins[f"in_{name}"] = np.ascontiguousarray(a)
        args.append(nc.dram_tensor(f"in_{name}", ins[f"in_{name}"].shape, F32, kind="ExternalInput").ap())
    out = nc.dram_tensor("out_y", (P, KT, SEQ), F32, kind="ExternalOutput").ap()
    build(nc, *args, out)
    r = run_bass_kernel_spmd(nc, [ins], core_ids=[0])
    y = np.asarray(r.results[0]["out_y"])
    return y.transpose(2, 1, 0).reshape(1, SEQ, D)
```
